# Optimizing a Trainium2 kernel written in Bass

```python
import math
import jax, jax.numpy as jnp
from jax import lax
import numpy as np

D_MODEL = 1024
BATCH = 1
SEQ = 512
DEPTH = 2
DEC_BATCH = 8
DEC_SEQ = 8
PAST_LEN = 2048
PAGE_SIZE = 128

N_MIXERS = 2
N_CONV_LAYERS = (DEPTH + 1) // 2
N_NSA_LAYERS = DEPTH // 2
EXPAND = 2
D_IN = EXPAND * D_MODEL
CONV_W = 31
N_HEADS = 16
HEAD_DIM = D_MODEL // N_HEADS
N_KV = 4
GROUP = N_HEADS // N_KV
ATT_W = N_HEADS * HEAD_DIM
KV_W = N_KV * HEAD_DIM
N_KV_STREAMS = 6
NSA_IN = 2 * ATT_W + N_KV_STREAMS * KV_W + 3 * N_HEADS
CMP_BLOCK = 32
CMP_STRIDE = 16
CMP_HID = 2 * HEAD_DIM
SEL_BLOCK = 64
N_SELECT = 16
WINDOW = 512
Q_BLOCK = 64
ALPHA = (2 * DEPTH) ** 0.25
BETA = (8 * DEPTH) ** -0.25
LN_EPS = 1e-5

kernel_name = "nsa_conformer_hybrid_step"

def layer_norm(x, g, b):
    xf = x.astype(jnp.float32)
    mu = jnp.mean(xf, axis=-1, keepdims=True)
    var = jnp.mean(jnp.square(xf - mu), axis=-1, keepdims=True)
    return ((xf - mu) * lax.rsqrt(var + LN_EPS)).astype(x.dtype) * g + b

def masked_softmax(s, mask):
    s = jnp.where(mask, s, -jnp.inf)
    m = jnp.max(s, axis=-1, keepdims=True)
    m = jnp.where(jnp.isfinite(m), m, 0.0)
    e = jnp.where(mask, jnp.exp(s - m), 0.0)
    return e / jnp.maximum(jnp.sum(e, axis=-1, keepdims=True), 1e-30)

def conv_mixer(x, state, w_in, b_in, dw_w, dw_b, ln_g, ln_b, w_out):
    h = x @ w_in + b_in
    a, gl, z = jnp.split(h, 3, axis=-1)
    u = a * jax.nn.sigmoid(gl)
    if state is None:
        up = jnp.pad(u, ((0, 0), (CONV_W - 1, 0), (0, 0)))
    else:
        up = jnp.concatenate([state, u], axis=1)
    new_state = up[:, up.shape[1] - (CONV_W - 1):]
    y = lax.conv_general_dilated(up, dw_w[:, None, :], window_strides=(1,), padding="VALID",
                                 dimension_numbers=("NWC", "WIO", "NWC"),
                                 feature_group_count=D_IN) + dw_b
    y = layer_norm(y, ln_g, ln_b)
    y = jax.nn.silu(y) * jax.nn.silu(z)
    return y @ w_out, new_state

def compress(kseq, pe, w1, b1, w2):
    B, L = kseq.shape[:2]
    r = CMP_BLOCK // CMP_STRIDE
    nchunk = L // CMP_STRIDE
    chunks = kseq[:, :nchunk * CMP_STRIDE].reshape(B, nchunk, CMP_STRIDE, N_KV, HEAD_DIM)
    w1r = w1.reshape(r, CMP_STRIDE, HEAD_DIM, CMP_HID)
    parts = jnp.einsum("bcsgd,jsdh->jbcgh", chunks, w1r)
    nc = nchunk - r + 1
    h = jnp.einsum("sd,sdh->h", pe, w1) + b1
    for j in range(r):
        h = h + parts[j][:, j:j + nc]
    return jnp.einsum("bcgh,hd->bcgd", jax.nn.silu(h), w2)

def cmp_to_sel(imp, n_sel):
    r = SEL_BLOCK // CMP_STRIDE
    lo = -(CMP_BLOCK // CMP_STRIDE - 1)
    nc = imp.shape[-1]
    p = jnp.pad(imp, [(0, 0)] * (imp.ndim - 1) + [(-lo, r * n_sel - nc)])
    out = 0.0
    for o in range(lo, r):
        start = o * CMP_STRIDE
        ov = max(0, min(SEL_BLOCK, start + CMP_BLOCK) - max(0, start))
        if ov == 0:
            continue
        out = out + (ov / CMP_BLOCK) * p[..., o - lo:o - lo + r * (n_sel - 1) + 1:r]
    return out

def nsa_attend(q, gates, pos_q, kc, vc, ksb, vsb, kw, vw, pos_w):
    B, Q = q.shape[:2]
    scale = HEAD_DIM ** -0.5
    t = pos_q[:, None]
    nc = kc.shape[1]
    cmp_end = jnp.arange(nc, dtype=jnp.int32) * CMP_STRIDE + CMP_BLOCK - 1
    m_cmp = (cmp_end[None, :] <= t)[None, :, None, None, :]
    s = jnp.einsum("bqgrd,bngd->bqgrn", q, kc).astype(jnp.float32) * scale
    p_cmp = masked_softmax(s, m_cmp)
    o_cmp = jnp.einsum("bqgrn,bngd->bqgrd", p_cmp.astype(vc.dtype), vc)
    n_sel = ksb.shape[2]
    imp = cmp_to_sel(jnp.sum(p_cmp, axis=3), n_sel)
    blk = jnp.arange(n_sel, dtype=jnp.int32)[None, :]
    cur = (pos_q // SEL_BLOCK)[:, None]
    causal = (blk <= cur)[None, :, None, :]
    forced = ((blk == 0) | (blk == cur) | (blk == cur - 1))[None, :, None, :]
    score = jnp.where(forced, jnp.inf, jnp.where(causal, imp, -jnp.inf))
    k_top = min(N_SELECT, n_sel)
    vals, idx = lax.top_k(score, k_top)
    blk_ok = vals > -jnp.inf
    bi = jnp.arange(B)[:, None, None, None]
    gi = jnp.arange(N_KV)[None, None, :, None]
    kg = ksb[bi, gi, idx]
    vg = vsb[bi, gi, idx]
    tok = idx[..., None] * SEL_BLOCK + jnp.arange(SEL_BLOCK, dtype=jnp.int32)
    m_sel = blk_ok[..., None] & (tok <= pos_q[None, :, None, None, None])
    m_sel = m_sel.reshape(B, Q, N_KV, 1, k_top * SEL_BLOCK)
    s = jnp.einsum("bqgrd,bqgksd->bqgrks", q, kg).astype(jnp.float32) * scale
    p = masked_softmax(s.reshape(B, Q, N_KV, GROUP, k_top * SEL_BLOCK), m_sel)
    p = p.reshape(B, Q, N_KV, GROUP, k_top, SEL_BLOCK).astype(vg.dtype)
    o_sel = jnp.einsum("bqgrks,bqgksd->bqgrd", p, vg)
    dpos = t - pos_w[None, :]
    m_win = ((dpos >= 0) & (dpos < WINDOW) & (pos_w[None, :] >= 0))[None, :, None, None, :]
    s = jnp.einsum("bqgrd,bsgd->bqgrs", q, kw).astype(jnp.float32) * scale
    p = masked_softmax(s, m_win)
    o_win = jnp.einsum("bqgrs,bsgd->bqgrd", p.astype(vw.dtype), vw)
    return gates[..., 0:1] * o_cmp + gates[..., 1:2] * o_sel + gates[..., 2:3] * o_win

def nsa_project(x, w_in):
    B, T, _ = x.shape
    h = x @ w_in
    o1 = ATT_W
    o2 = o1 + N_KV_STREAMS * KV_W
    o3 = o2 + 3 * N_HEADS
    q = h[..., :o1].reshape(B, T, N_KV, GROUP, HEAD_DIM)
    kv = h[..., o1:o2].reshape(B, T, N_KV_STREAMS, N_KV, HEAD_DIM)
    gates = jax.nn.sigmoid(h[..., o2:o3].reshape(B, T, N_KV, GROUP, 3))
    z = h[..., o3:]
    return q, kv, gates, z

def branch_keys(seq, pe, w1, b1, w2):
    B, L = seq.shape[:2]
    kc = compress(seq[:, :, 0], pe[0], w1[0], b1[0], w2[0])
    vc = compress(seq[:, :, 1], pe[1], w1[1], b1[1], w2[1])
    sel = seq[:, :, 2:].reshape(B, L // SEL_BLOCK, SEL_BLOCK, 2, N_KV, HEAD_DIM)
    sel = sel.transpose(3, 0, 4, 1, 2, 5)
    return kc, vc, sel[0], sel[1]

def nsa_output(o, z, w_out):
    B, T = o.shape[:2]
    return (o.reshape(B, T, ATT_W) * jax.nn.silu(z)) @ w_out

def nsa_prompt(x, w_in, pe, w1, b1, w2, w_out):
    B, T, _ = x.shape
    q, kv, gates, z = nsa_project(x, w_in)
    rows, win = kv[:, :, :4], kv[:, :, 4:]
    kc, vc, ksb, vsb = branch_keys(rows, pe, w1, b1, w2)
    wpad = jnp.pad(win, ((0, 0), (WINDOW, 0), (0, 0), (0, 0), (0, 0)))

    def block(i):
        qs = i * Q_BLOCK
        qb = lax.dynamic_slice_in_dim(q, qs, Q_BLOCK, axis=1)
        gb = lax.dynamic_slice_in_dim(gates, qs, Q_BLOCK, axis=1)
        wb = lax.dynamic_slice_in_dim(wpad, qs, WINDOW + Q_BLOCK, axis=1)
        pos_q = qs + jnp.arange(Q_BLOCK, dtype=jnp.int32)
        pos_w = qs - WINDOW + jnp.arange(WINDOW + Q_BLOCK, dtype=jnp.int32)
        return nsa_attend(qb, gb, pos_q, kc, vc, ksb, vsb, wb[:, :, 0], wb[:, :, 1], pos_w)

    o = lax.map(block, jnp.arange(T // Q_BLOCK, dtype=jnp.int32))
    o = jnp.moveaxis(o, 0, 1).reshape(B, T, N_KV, GROUP, HEAD_DIM)
    return nsa_output(o, z, w_out), rows, win[:, T - min(WINDOW, T):]

def nsa_sample(x, cache_kv_l, cache_win_l, page_table, w_in, pe, w1, b1, w2, w_out):
    B, T, _ = x.shape
    q, kv, gates, z = nsa_project(x, w_in)
    rows, win = kv[:, :, :4], kv[:, :, 4:]
    past_len = page_table.shape[1] * cache_kv_l.shape[1]
    past = cache_kv_l[page_table].reshape(B, past_len, 4, N_KV, HEAD_DIM)
    n_pad = (-T) % SEL_BLOCK
    seq = jnp.concatenate([past, rows, jnp.zeros((B, n_pad) + rows.shape[2:], rows.dtype)], axis=1)
    kc, vc, ksb, vsb = branch_keys(seq, pe, w1, b1, w2)
    wbuf = cache_win_l.shape[1]
    wseq = jnp.concatenate([cache_win_l, win], axis=1)
    pos_w = past_len - wbuf + jnp.arange(wbuf + T, dtype=jnp.int32)
    pos_q = past_len + jnp.arange(T, dtype=jnp.int32)
    o = nsa_attend(q, gates, pos_q, kc, vc, ksb, vsb, wseq[:, :, 0], wseq[:, :, 1], pos_w)
    return nsa_output(o, z, w_out), rows, wseq[:, T:]

def setup_inputs(seed: int = 0) -> dict:
    key = jax.random.key(seed)
    ks = jax.random.split(key, 24)
    n_pages = PAST_LEN // PAGE_SIZE
    n_used = DEC_BATCH * n_pages
    n_pool = n_used + n_used // 4
    win_buf = min(WINDOW, PAST_LEN)
    f32 = jnp.float32

    def nrm(k, shape, s):
        return jax.random.normal(k, shape, f32) * s

    page_table = jax.random.permutation(ks[5], n_pool)[:n_used].reshape(DEC_BATCH, n_pages).astype(jnp.int32)
    return {
        "x_prompt": nrm(ks[0], (BATCH, SEQ, D_MODEL), 1.0),
        "x_sample": nrm(ks[1], (DEC_BATCH, DEC_SEQ, D_MODEL), 1.0),
        "state_conv": nrm(ks[2], (N_CONV_LAYERS, DEC_BATCH, CONV_W - 1, D_IN), 0.5),
        "cache_kv": nrm(ks[3], (N_NSA_LAYERS, n_pool, PAGE_SIZE, 4, N_KV, HEAD_DIM), 1.0),
        "cache_win": nrm(ks[4], (N_NSA_LAYERS, DEC_BATCH, win_buf, 2, N_KV, HEAD_DIM), 1.0),
        "page_table": page_table,
        "conv_w_in": nrm(ks[6], (N_CONV_LAYERS, D_MODEL, 3 * D_IN), D_MODEL ** -0.5),
        "conv_b_in": nrm(ks[7], (N_CONV_LAYERS, 3 * D_IN), 0.02),
        "conv_dw_w": nrm(ks[8], (N_CONV_LAYERS, CONV_W, D_IN), CONV_W ** -0.5),
        "conv_dw_b": nrm(ks[9], (N_CONV_LAYERS, D_IN), 0.02),
        "conv_ln_g": 1.0 + nrm(ks[10], (N_CONV_LAYERS, D_IN), 0.02),
        "conv_ln_b": nrm(ks[11], (N_CONV_LAYERS, D_IN), 0.02),
        "conv_w_out": nrm(ks[12], (N_CONV_LAYERS, D_IN, D_MODEL), BETA * D_IN ** -0.5),
        "nsa_w_in": nrm(ks[13], (N_NSA_LAYERS, D_MODEL, NSA_IN), D_MODEL ** -0.5),
        "cmp_pe": nrm(ks[14], (N_NSA_LAYERS, 2, CMP_BLOCK, HEAD_DIM), 0.1),
        "cmp_w1": nrm(ks[15], (N_NSA_LAYERS, 2, CMP_BLOCK, HEAD_DIM, CMP_HID), (CMP_BLOCK * HEAD_DIM) ** -0.5),
        "cmp_b1": nrm(ks[16], (N_NSA_LAYERS, 2, CMP_HID), 0.02),
        "cmp_w2": nrm(ks[17], (N_NSA_LAYERS, 2, CMP_HID, HEAD_DIM), CMP_HID ** -0.5),
        "nsa_w_out": nrm(ks[18], (N_NSA_LAYERS, ATT_W, D_MODEL), BETA * ATT_W ** -0.5),
        "ln_g": 1.0 + nrm(ks[19], (DEPTH, D_MODEL), 0.02),
        "ln_b": nrm(ks[20], (DEPTH, D_MODEL), 0.02),
    }

def reference(x_prompt, x_sample, state_conv, cache_kv, cache_win, page_table,
              conv_w_in, conv_b_in, conv_dw_w, conv_dw_b, conv_ln_g, conv_ln_b, conv_w_out,
              nsa_w_in, cmp_pe, cmp_w1, cmp_b1, cmp_w2, nsa_w_out, ln_g, ln_b):
    xp, xs = x_prompt, x_sample
    conv_p, conv_s, kv_p, kv_s, win_p, win_s = [], [], [], [], [], []
    for i in range(DEPTH):
        j = i // N_MIXERS
        if i % N_MIXERS == 0:
            cw = (conv_w_in[j], conv_b_in[j], conv_dw_w[j], conv_dw_b[j],
                  conv_ln_g[j], conv_ln_b[j], conv_w_out[j])
            yp, sp = conv_mixer(xp, None, *cw)
            ys, ss = conv_mixer(xs, state_conv[j], *cw)
            conv_p.append(sp)
            conv_s.append(ss)
        else:
            nw = (nsa_w_in[j], cmp_pe[j], cmp_w1[j], cmp_b1[j], cmp_w2[j], nsa_w_out[j])
            yp, rp, wp = nsa_prompt(xp, *nw)
            ys, rs, ws = nsa_sample(xs, cache_kv[j], cache_win[j], page_table, *nw)
            kv_p.append(rp)
            kv_s.append(rs)
            win_p.append(wp)
            win_s.append(ws)
        xp = layer_norm(ALPHA * xp + yp, ln_g[i], ln_b[i])
        xs = layer_norm(ALPHA * xs + ys, ln_g[i], ln_b[i])
    return (xp, xs, jnp.stack(conv_p), jnp.stack(conv_s), jnp.stack(kv_p), jnp.stack(kv_s),
            jnp.stack(win_p), jnp.stack(win_s))


_drawn_inputs = setup_inputs


def setup_inputs(seed=0):
    import zlib

    import numpy as np

    out = dict(_drawn_inputs(seed))
    spreads = {}
    factors = {'cache_kv': 6.347,
     'conv_dw_b': 8.0,
     'conv_ln_g': 8.0,
     'conv_ln_b': 8.0,
     'cmp_pe': 8.0,
     'cmp_b1': 8.0}
    for name, (base, spread) in spreads.items():
        noise = np.random.default_rng([zlib.crc32(name.encode()), seed]).standard_normal(out[name].shape)
        drawn = base * np.exp(spread * noise) if base else spread * noise
        out[name] = __import__('jax').numpy.asarray(drawn.astype(out[name].dtype))
    for name, factor in factors.items():
        out[name] = (out[name] * factor).astype(out[name].dtype)
    return out
```

```python
from contextlib import ExitStack

import concourse.bass as bass
from concourse import mybir

F32 = mybir.dt.float32
I32 = mybir.dt.int32
ALU = mybir.AluOpType
ACT = mybir.ActivationFunctionType
AX = mybir.AxisListType.X

P = 128
DM = 1024
KT = DM // P
DIN = 2048
CT = DIN // P
TAPS = 31
TP = 512
NB, TS = 8, 8
TOK = TP + NB * TS
HALF = TOK // 2
TT = 5
ROWS = [P, P, P, P, NB * TS]
HD = 64
NH = 16
NKV = 4
GRP = NH // NKV
PAST = 2048
PAGE = 128
NPG = PAST // PAGE
STR = 16
SP2 = STR // 2
NC = PAST // STR - 1
PC = TP // STR
PCN = PC - 1
NSEL = 33
BLK = 64
WIN = 512
ALPHA = (2 * 2) ** 0.25
EPS = 1e-5
NEG = -1.0e30
BIG = 3.0e38
RING = 8
NPAR = TAPS + 6
UPS = TS + TAPS - 1
CONV_AHEAD = TAPS - 1
ARENA = 53056


UNITS = [(g2, i, br, c) for c in range(2) for g2 in range(2) for i in range(TP // P) for br in range(2)]


class Chain:

    def __init__(self, eng, sem):
        self.eng, self.sem, self.base, self.n = eng, sem, 0, 0

    def mark(self, ins):
        ins.then_inc(self.sem, 1)
        self.n += 1
        return self.base + self.n

    def link(self, ins):
        self.eng.wait_ge(self.sem, self.mark(ins))

    def enter(self, base):
        self.base, self.n = base, 0


def build_program(nc, x_prompt, x_sample, state_conv, cache_kv, cache_win, page_table,
                  conv_w_in, conv_b_in, conv_dw_w, conv_dw_b, conv_ln_g, conv_ln_b, conv_w_out,
                  nsa_w_in, cmp_pe, cmp_w1, cmp_b1, cmp_w2, nsa_w_out, ln_g, ln_b,
                  y_prompt, y_sample, state_p, state_s, kv_p, kv_s, win_p, win_s):
    ctx = ExitStack()
    with ctx:
        def sem(name):
            return ctx.enter_context(nc.semaphore(name))

        arena = ctx.enter_context(nc.sbuf_tensor("arena", [P, ARENA], F32))
        pages = ctx.enter_context(nc.sbuf_tensor("pages", [1, NB * NPG], I32))
        bank = [ctx.enter_context(nc.psum_tensor(f"bank{i}", [P, 512], F32)) for i in range(8)]

        def at(kib, n):
            o = int(kib * 256)
            assert o + n <= ARENA
            return arena[:, o:o + n]

        xr = at(0, TT * DM).rearrange("p (t m) -> p t m", t=TT)
        xT = at(20, KT * TOK).rearrange("p (k t) -> p k t", k=KT)
        kcT = at(38, NB * 2 * NC).rearrange("p (b g n) -> p b g n", b=NB, g=2)
        vc = at(46, NB * 256).rearrange("p (b v) -> p b v", b=NB)
        ident = at(54, P)
        tri = at(54.5, P)
        quad = at(55, P)
        wmask = at(55.5, WIN + TS)
        cmask = at(57.75, 4 * PC).rearrange("p (i n) -> p i n", i=4)
        cvalid = at(58.25, 4)
        w2pad = at(58.5, 2 * P).rearrange("p (g m) -> p g m", g=2)
        w2v = at(59.5, HD)
        auxT = at(59.75, 34)
        cb = at(60, 2)
        par = at(60.25, 2 * NPAR).rearrange("p (c n) -> p c n", c=2)
        pars = at(61, CT * NPAR).rearrange("p (c n) -> p c n", c=CT)
        uo = at(63.5, 2 * 256).rearrange("p (c m) -> p c m", c=2)
        stat = at(65.5, 128)
        gain = at(66, DM)
        offs = at(70, DM)
        wc = at(74, 32 * P).rearrange("p (s j q h) -> p s j q h", s=2, j=2, q=SP2)

        xc = at(90, 2 * 8192).rearrange("p (c s f) -> p c s f", c=2, s=STR)
        rl = at(154, 2 * 4096).rearrange("p (s g q n) -> p s g q n", s=2, g=NKV, q=SP2)
        xtr = at(186, 4 * 512).rearrange("p (c n) -> p c n", c=4)
        hT = at(194, 2 * 512).rearrange("p (c n) -> p c n", c=2)
        aux2 = at(199, P)
        ones = at(206.75, P)

        y = at(114, CT * TOK).rearrange("p (c t) -> p c t", c=CT)
        sz = at(150, CT * TOK).rearrange("p (c t) -> p c t", c=CT)
        wi = at(90, 2 * 3 * KT * P).rearrange("p (c a k n) -> p c a k n", c=2, a=3, k=KT)
        ring = at(90, RING * 512).rearrange("p (r n) -> p r n", r=RING)
        aux = at(191, DIN)
        up = at(191, 2 * 880).rearrange("p (c n) -> p c n", c=2)
        upp = [up[:, c, 0:CONV_AHEAD + TP] for c in range(2)]
        ups = [up[:, c, CONV_AHEAD + TP:CONV_AHEAD + TP + NB * UPS].rearrange("p (b n) -> p b n", b=NB)
               for c in range(2)]
        usc = at(65.5, 2 * 64).rearrange("p (c n) -> p c n", c=2)
        sgl = at(198, TOK)
        acc = at(200.25, TOK)
        sgz = at(202.5, TOK)
        st = at(204.75, 2 * 2 * P).rearrange("p (c h m) -> p c h m", c=2, h=2)
        sq = [sgl, sgz]

        qT = at(106, KT * TOK).rearrange("p (m t) -> p m t", m=8)
        kvr = at(124, TT * 1536).rearrange("p (t n) -> p t n", t=TT)
        zr = at(154, TT * DM).rearrange("p (t n) -> p t n", t=TT)
        gates = at(174, TT * 48).rearrange("p (t h j) -> p t h j", t=TT, j=3)
        ktp = at(175, 4 * TP).rearrange("p (s g n) -> p s g n", s=2, g=2)
        sig = at(186, 2 * 512).rearrange("p (c n) -> p c n", c=2)
        kts = at(194, 4 * 64).rearrange("p (s g n) -> p s g n", s=2, g=2)
        zts = at(195, 8 * 64).rearrange("p (m n) -> p m n", m=8)
        qbd = at(197, NB * 256).rearrange("p (b g n) -> p b g n", b=NB, g=2)
        gs = at(205, NB * 3).rearrange("p (b j) -> p b j", b=NB)
        rlp = [v.rearrange("p (g q n) -> p g q n", g=NKV, q=SP2) for v in (at(20, 4096), at(90, 4096))]
        xtp = at(197, 16 * P).rearrange("p (k g n) -> p k g n", k=16, g=NKV)
        htp = at(190, 2 * P).rearrange("p (s n) -> p s n", s=2)
        kctp = at(191, 4 * PC).rearrange("p (a g n) -> p a g n", a=2, g=2)
        vcp = at(192, 256)
        vbd = at(66, 4 * 256).rearrange("p (g n) -> p g n", g=NKV)

        att = at(20, 4 * DM).rearrange("p (i m g d) -> p i m g d", i=4, m=8, g=2)
        qs = [at(k, 2 * TP).rearrange("p (g n) -> p g n", g=2) for k in (186, 70)]
        prob = at(74, 3 * 512).rearrange("p (c n) -> p c n", c=3)
        probT = at(80, 2 * 512).rearrange("p (c n) -> p c n", c=2)
        pc = at(84, 512)
        pcT = at(86, 512)
        cst = at(88, 64)
        ust = at(88.5, 64)
        oT = at(106, KT * TOK).rearrange("p (m t) -> p m t", m=8)

        kv = at(124, 2 * 8192).rearrange("p (c n f) -> p c n f", c=2, n=NPG)
        wk = at(90, 2 * 2048).rearrange("p (c n f) -> p c n f", c=2, n=4)
        pb = [at(20, 2703), at(74, 2703)]
        ktb = [at(k, 1024).rearrange("p (g n) -> p g n", g=2) for k in (31, 85)]
        pt = at(66, 4 * 512).rearrange("p (c n) -> p c n", c=4)
        qb = at(35, 2 * 256).rearrange("p (c g n) -> p c g n", c=2, g=2)
        vcb = at(188, 2 * 256).rearrange("p (c n) -> p c n", c=2)
        vn = at(190, 2 * 512).rearrange("p (c s n) -> p c s n", c=2, s=2)
        pcn = at(37, NC)
        sel = at(37.5, 128)
        sst = at(205.25, 64)
        q7 = at(205.5, 30)
        ring2 = at(124, RING * 512).rearrange("p (r n) -> p r n", r=RING)
        gate_rows = nc.dram_tensor("gate_rows", (NB * TS, 48), F32, kind="Internal").ap()

        s_bank = [bank[n] for n in (1, 2, 7, 1, 2)]

        def split(v):
            return v[:, 0:TP], v[:, TP:TOK]

        block = ctx.enter_context(nc.Block())

        s_const = sem("s_const")
        s_small = sem("s_small")
        s_x = sem("s_x")
        s_wc = sem("s_wc")
        s_cpy = sem("s_cpy")
        s_xps = sem("s_xps")
        s_xev = [sem(f"s_xev{w}") for w in range(2)]
        s_aps = sem("s_aps")
        s_aev = sem("s_aev")
        s_cbp = sem("s_cbp")
        s_cb = sem("s_cb")
        s_pg = sem("s_pg")
        xc_in = [sem(f"xc_in{c}") for c in range(2)]
        rl_ready = sem("rl_ready")
        xp_ready = sem("xp_ready")
        xt_v = sem("xt_v")
        xt_a = sem("xt_a")
        xt_used = sem("xt_used")
        h_silu = sem("h_silu")
        kc_ps = sem("kc_ps")
        vc_ps = sem("vc_ps")
        kc_ev = sem("kc_ev")
        vc_ev = sem("vc_ev")
        wi_in = [sem(f"wi_in{c}") for c in range(2)]
        gl_ps = sem("gl_ps")
        a_ps = sem("a_ps")
        z_ps = sem("z_ps")
        gl_free = sem("gl_free")
        a_free = sem("a_free")
        z_free = sem("z_free")
        sgz_ready = sem("sgz_ready")
        par_ready = sem("par_ready")
        st_ps = sem("st_ps")
        st_up = sem("st_up")
        u_ps = sem("u_ps")
        uo_ready = sem("uo_ready")
        state_out = [sem(f"state_out{c}") for c in range(2)]
        conv_done = sem("conv_done")
        sq_ready = sem("sq_ready")
        sq_used = sem("sq_used")
        var_ready = sem("var_ready")
        std_ready = sem("std_ready")
        norm_done = sem("norm_done")
        yn_act = sem("yn_act")
        yn_ready = sem("yn_ready")
        ring_in = [sem(f"ring_in{r}") for r in range(RING)]
        ring_used = sem("ring_used")
        o_ps = sem("o_ps")
        o_free = sem("o_free")
        s_ln = sem("s_ln")
        kv_ps = sem("kv_ps")
        kv_ev = sem("kv_ev")
        kv_out = sem("kv_out")
        q_ev_a = sem("q_ev_a")
        q_ev_v = sem("q_ev_v")
        q_ps = sem("q_ps")
        zz_ps = sem("zz_ps")
        zz_sg = sem("zz_sg")
        zz_ev = sem("zz_ev")
        g_ps = sem("g_ps")
        g_ev = sem("g_ev")
        gr_out = sem("gr_out")
        gr_in = sem("gr_in")
        kt_ps = sem("kt_ps")
        kt_ev = sem("kt_ev")
        rlp_in = sem("rlp_in")
        xtp_ps = sem("xtp_ps")
        xtp_ev_v = sem("xtp_ev_v")
        xtp_ev_a = sem("xtp_ev_a")
        hp_ps = sem("hp_ps")
        hp_ev = sem("hp_ev")
        w2p_ps = sem("w2p_ps")
        w2p_ev = sem("w2p_ev")
        vbd_zero = sem("vbd_zero")
        vbd_in = sem("vbd_in")
        xtp_done = sem("xtp_done")
        qbd_ready = sem("qbd_ready")
        cs_ps = sem("cs_ps")
        cs_mx = sem("cs_mx")
        cs_ex = sem("cs_ex")
        cs_sc = sem("cs_sc")
        ct_ps = sem("ct_ps")
        ct_ev = sem("ct_ev")
        co_ps = sem("co_ps")
        co_ev = sem("co_ev")
        u_sc = sem("u_sc")
        u_mx = sem("u_mx")
        u_ex = sem("u_ex")
        u_tp = sem("u_tp")
        u_pt = sem("u_pt")
        u_pv = sem("u_pv")
        u_fo = sem("u_fo")
        qs_ready = sem("qs_ready")
        oz_ready = sem("oz_ready")
        oT_ps = sem("oT_ps")
        e_stage = sem("e_stage")
        e_used = sem("e_used")
        e_sc = sem("e_sc")
        e_cm = sem("e_cm")
        e_cx = sem("e_cx")
        e_cn = sem("e_cn")
        e_q4 = sem("e_q4")
        e_tp = sem("e_tp")
        e_te = sem("e_te")
        e_s = sem("e_s")
        e_ma = sem("e_ma")
        e_nm = sem("e_nm")
        e_ex = sem("e_ex")
        e_scl = sem("e_scl")
        e_pp = sem("e_pp")
        e_pt_v = sem("e_pt_v")
        e_pt_a = sem("e_pt_a")
        e_pv = sem("e_pv")
        e_pv_done = sem("e_pv_done")
        e_oz = sem("e_oz")
        vn_in = sem("vn_in")
        oT_ev = [sem(f"oT_ev{w}") for w in range(2)]
        x1_ev = [sem(f"x1_ev{w}") for w in range(2)]
        x1_ps = sem("x1_ps")
        win_in = [sem(f"win_in{c}") for c in range(2)]
        kt_ev_a = sem("kt_ev_a")
        kv_in = [sem(f"kv_in{c}") for c in range(2)]
        v_in = [sem(f"v_in{c}") for c in range(2)]
        q_stage = sem("q_stage")
        c_stage = sem("c_stage")
        ring2_in = [sem(f"ring2_in{r}") for r in range(RING)]
        ring2_used = sem("ring2_used")
        o2_ps = sem("o2_ps")
        ln_done = sem("ln_done")
        dve_s = sem("dve_s")
        act_s = sem("act_s")
        pool_s = sem("pool_s")

        def transposed_copy(eng, t, who, ps, ev, dst):
            n = ROWS[t]
            eng.wait_ge(ps, t + 1)
            src = bank[(2 * t) % 4 + who][:, :].rearrange("p (k n) -> p k n", k=4)[:, :, 0:n]
            (eng.copy if who else eng.tensor_copy)(dst[:, 4 * who:4 * who + 4, t * P:t * P + n], src).then_inc(ev[who], 1)

        def transpose_tiles(pe, src, tiles, ps, ev, ready=None):
            for t in range(tiles):
                n = ROWS[t]
                if ready is not None:
                    pe.wait_ge(ready, t + 1)
                for k in range(KT):
                    if t >= 2 and k % 4 == 0:
                        pe.wait_ge(ev[k // 4], t - 1)
                    last = pe.transpose(bank[(2 * t) % 4 + k // 4][:, (k % 4) * P:(k % 4) * P + n], src(t, k)[0:n],
                                        ident[0:n, 0:n])
                last.then_inc(ps, 1)

        def token_product(pe, lhs, k, slot, width, first, last_k, free, ready):
            for t in range(TT):
                r = ROWS[t]
                if first:
                    free(t)
                ins = pe.matmul(bank[t][0:r, 0:width], lhs(k, t), slot, start=first, stop=last_k)
                if last_k and t < TT - 1:
                    ins.then_inc(ready, 1)
            return ins

        def sample_order(eng, first, soften, second, ch=None):
            c0 = (ch.base + ch.n) if ch else 0
            first(0, 0)
            for step in soften(0, 0):
                step()
            per = (ch.base + ch.n - c0) if ch else 0
            with eng.Fori(0, NB // 2 - 1) as it:
                for c in range(2):
                    if ch:
                        ch.enter(it * (2 * per) + (c0 + per * (c + 1)))
                    first(it * 2 + (1 + c), 1 - c)
                    second(it * 2 + c, c, soften(it * 2 + (1 + c), 1 - c))
                    assert not ch or ch.n == per
            if ch:
                ch.enter(c0 + per * (NB - 1))
            first(NB - 1, 1)
            second(NB - 2, 0, soften(NB - 1, 1))
            second(NB - 1, 1, [])

        def staging_order(eng, keys, values):
            keys(0, 0)
            keys(1, 1)
            values(0, 0)
            values(1, 1)
            keys(2, 0)
            with eng.Fori(1, NB // 2 - 1) as it:
                keys(it * 2 + 1, 1)
                values(it * 2, 0)
                keys(it * 2 + 2, 0)
                values(it * 2 + 1, 1)
            keys(NB - 1, 1)
            values(NB - 2, 0)
            values(NB - 1, 1)

        def layer_norm(dve, ch, before, loaded, layer):
            dve.wait_ge(o_free, before)
            dve.wait_ge(s_ln, loaded)
            ch.link(dve.memset(stat[:, 64:80], 1.0))
            for t in range(TT):
                n = ROWS[t]
                st6 = stat[0:n, 12 * t:12 * t + 12].rearrange("p (c s) -> p c s", c=2)
                for h in range(2):
                    ch.mark(dve.bn_stats(st6[:, h], xr[0:n, t, h * 512:(h + 1) * 512]))
                dve.wait_ge(dve_s, ch.base + ch.n)
                ch.mark(dve.bn_aggr(stat[0:n, 64 + 2 * t:66 + 2 * t], st6))
            dve.wait_ge(dve_s, ch.base + ch.n)
            dve.tensor_scalar(stat[:, 80:85], stat[:, 65:75:2], EPS, None, ALU.add).then_inc(var_ready, 1)
            dve.wait_ge(std_ready, layer)
            ch.link(dve.reciprocal(stat[:, 96:101], stat[:, 88:93]))
            for t in range(TT):
                n = ROWS[t]
                row = xr[0:n, t]
                ch.link(dve.tensor_scalar(row, row, stat[0:n, 64 + 2 * t:65 + 2 * t], stat[0:n, 96 + t:97 + t],
                                          ALU.subtract, ALU.mult))
                ch.link(dve.tensor_tensor(row, row, gain[0:n], ALU.mult))
                dve.tensor_tensor(row, row, offs[0:n], ALU.add).then_inc(ln_done, 1)

        def deviations(act, layer):
            act.wait_ge(var_ready, layer)
            act.activation(stat[:, 88:93], stat[:, 80:85], ACT.Sqrt).then_inc(std_ready, 1)

        @block.sync
        def _(sp):
            sp.dma_start(xr[:, 0:4, :], x_prompt[0].rearrange("(t p) m -> p t m", p=P)).then_inc(s_x, 16)
            sp.dma_start(xr[0:64, 4, :], x_sample.rearrange("b t m -> (b t) m")).then_inc(s_x, 16)
            sp.dma_start(pages[:, :], page_table.rearrange("(o b) n -> o (b n)", o=1)).then_inc(s_pg, 16)
            sp.dma_start(aux2[0:32, :], cmp_pe[0].rearrange("s (q e) d -> (s q) (e d)", e=2)).then_inc(s_small, 16)
            sp.dma_start(aux2[32:34, :], cmp_b1[0]).then_inc(s_small, 16)
            for g in range(2):
                sp.dma_start(w2pad[:, g, g * HD:(g + 1) * HD], cmp_w2[0, 0]).then_inc(s_small, 16)
            sp.dma_start(w2v, cmp_w2[0, 1]).then_inc(s_small, 16)
            sp.dma_start(aux[0:TAPS, :], conv_dw_w[0]).then_inc(s_small, 16)
            sp.dma_start(aux[TAPS:TAPS + 3, :], conv_b_in[0].rearrange("(a n) -> a n", a=3)).then_inc(s_small, 16)
            for r, v in enumerate((conv_dw_b, conv_ln_g, conv_ln_b)):
                sp.dma_start(aux[TAPS + 3 + r:TAPS + 4 + r, :], v).then_inc(s_small, 16)
            for s in range(2):
                sp.dma_start(wc[:, s].rearrange("p j q h -> p (j q) h"),
                             cmp_w1[0, s].rearrange("(q e) d h -> (e d) q h", e=2)).then_inc(s_wc, 16)

            def load_chunks(it):
                for c in range(2):
                    for n in range(NPG):
                        pg = sp.value_load(pages[0:1, bass.ds((it * 2 + c) * NPG + n, 1)], min_val=0, max_val=cache_kv.shape[1] - 1)
                        if n == 0 and type(it) is not int:
                            sp.wait_ge(rl_ready, it * 4 + c * 2 - 2)
                        sp.dma_start(xc[n * 8:n * 8 + 8, c],
                                     cache_kv[0, bass.ds(pg, 1)].rearrange("o (c s) k g d -> (o c) s (k g d)", s=STR)[:, :, 0:512]
                                     ).then_inc(xc_in[c], 16)

            def load_mixer(it):
                for c in range(2):
                    for a in range(3):
                        if a == 0 and type(it) is not int:
                            sp.wait_ge(z_ps, it * 2 + c - 1)
                        sp.dma_start(wi[:, c, a],
                                     conv_w_in[0].rearrange("(k p) n -> p k n", p=P)[:, :, bass.ds(it * 256 + (a * DIN + c * P), P)]
                                     ).then_inc(wi_in[c], 16)
                    sp.dma_start(st[0:120, c],
                                 state_conv[0].rearrange("(h b) t n -> (b t) h n", h=2)[:, :, bass.ds(it * 256 + c * P, P)]
                                 ).then_inc(wi_in[c], 16)

            sp.wait_ge(s_pg, 16)
            load_chunks(0)
            with sp.Fori(1, NB // 2) as it:
                load_chunks(it)
            sp.wait_ge(rl_ready, 2 * NB)
            load_mixer(0)
            with sp.Fori(1, CT // 2) as it:
                load_mixer(it)
            sp.dma_start(gain, ln_g[0:1, :].broadcast_to([P, DM])).then_inc(s_ln, 16)
            sp.dma_start(offs, ln_b[0:1, :].broadcast_to([P, DM])).then_inc(s_ln, 16)
            sp.dma_start(state_s[0, :, 0:TAPS - 1 - TS].rearrange("b t n -> b (t n)"),
                         state_conv[0, :, TS:TAPS - 1].rearrange("b t n -> b (t n)")).then_inc(s_cpy, 16)
            sp.dma_start(win_s[0, :, 0:WIN - TS].rearrange("b t k g d -> b (t k g d)"),
                         cache_win[0, :, TS:WIN].rearrange("b t k g d -> b (t k g d)")).then_inc(s_cpy, 16)
            sp.wait_ge(z_ps, CT)
            for nh in range(2):
                for c in range(CT):
                    n = nh * CT + c
                    if n >= RING:
                        sp.wait_ge(ring_used, n - RING + 1)
                    sp.dma_start(ring[:, n % RING], conv_w_out[0, c * P:(c + 1) * P, nh * 512:(nh + 1) * 512]
                                 ).then_inc(ring_in[n % RING], 16)
            w_in = nsa_w_in[0]
            used = 2 * CT - RING
            with sp.Fori(0, 3) as it:
                for k in range(KT):
                    sp.wait_ge(ring_used, it * RING + (used + k + 1))
                    sp.dma_start(ring[:, k], w_in[k * P:(k + 1) * P, bass.ds(it * 512 + DM, 512)]).then_inc(ring_in[k], 16)

            def load_permuted(base, used):
                with sp.Fori(0, 2) as it:
                    for k in range(KT):
                        sp.wait_ge(ring_used, it * RING + (used + k + 1))
                        for g in range(2):
                            sp.dma_start(ring[:, k].rearrange("p (r g d) -> p g r d", r=GRP, g=2)[:, g],
                                         w_in[k * P:(k + 1) * P, bass.ds(it * 512 + (base + g * 256), 256)].rearrange(
                                             "p (r d) -> p r d", r=GRP)).then_inc(ring_in[k], 16)
            load_permuted(0, used + 24)
            load_permuted(2608, used + 40)
            for k in range(KT):
                sp.wait_ge(ring_used, used + 56 + k + 1)
                sp.dma_start(ring[:, k, 0:48], w_in[k * P:(k + 1) * P, 2560:2608]).then_inc(ring_in[k], 16)
            sp.wait_ge(g_ev, TT)
            sp.dma_start(gate_rows, gates[0:64, 4].rearrange("p h j -> p (h j)")).then_inc(gr_out, 16)
            sp.wait_ge(kv_out, 64)
            for st_ in range(2):
                for g in range(NKV):
                    sp.dma_start(rlp[st_][0:PC, g].rearrange("p q (e d) -> p (q e) d", e=2),
                                 kv_p[0, 0, :, st_, g].rearrange("(c t) d -> c t d", t=STR)).then_inc(rlp_in, 16)
            sp.wait_ge(gr_out, 16)
            sp.dma_start(gs, gate_rows.rearrange("(b q) (h j) -> (q h) b j", b=NB, j=3)).then_inc(gr_in, 16)
            sp.wait_ge(w2p_ev, 3)
            sp.wait_ge(vbd_zero, 1)
            for r in range(GRP):
                sp.dma_start(vbd[32 * r:32 * r + PCN, :, r * HD:(r + 1) * HD], vcp[0:PCN].rearrange("p (g d) -> p g d", g=NKV)
                             ).then_inc(vbd_in, 16)
            def window_keys(b, c):
                sp.dma_start(wk[:, c, :, 0:256], cache_win[0, bass.ds(b, 1), :, 0].rearrange("o (n p) g d -> p (o n) (g d)", p=P)
                             ).then_inc(win_in[c], 16)

            def window_values(b, c):
                sp.dma_start(wk[:, c, :, 256:512], cache_win[0, bass.ds(b, 1), :, 1].rearrange("o (n p) g d -> p (o n) (g d)", p=P)
                             ).then_inc(v_in[c], 16)
                sp.dma_start(vn[0:TS, c, 0], kv_s[0, bass.ds(b, 1), :, 3].rearrange("o t g d -> (o t) (g d)")).then_inc(v_in[c], 16)
                sp.dma_start(vn[0:TS, c, 1], win_s[0, bass.ds(b, 1), WIN - TS:WIN, 1].rearrange("o t g d -> (o t) (g d)")
                             ).then_inc(v_in[c], 16)

            def load_pages(b, c, half, ready):
                for n in range(NPG):
                    pg = sp.value_load(pages[0:1, bass.ds(b * NPG + n, 1)], min_val=0, max_val=cache_kv.shape[1] - 1)
                    sp.dma_start(kv[:, c, n, half * 256:(half + 1) * 256],
                                 cache_kv[0, bass.ds(pg, 1), :, 2 + half].rearrange("o t g d -> (o t) (g d)")).then_inc(ready, 16)

            def load_keys(b, c):
                if type(b) is not int or b >= 2:
                    sp.wait_ge(e_tp, b * 5 - 5)
                    window_keys(b, c)
                load_pages(b, c, 0, kv_in[c])

            def load_values(b, c):
                if type(b) is not int or b >= 2:
                    sp.wait_ge(e_pv, b - 1)
                    window_values(b, c)
                load_pages(b, c, 1, v_in[c])

            sp.wait_ge(co_ev, 8)
            for b in range(2):
                window_keys(b, b)
                window_values(b, b)
            sp.wait_ge(oz_ready, 4)
            sp.wait_ge(oT_ps, 4)
            staging_order(sp, load_keys, load_values)

            for nh in range(2):
                for m in range(8):
                    if nh == 0 and m == 0:
                        sp.wait_ge(e_pv, NB - 1)
                    if nh:
                        sp.wait_ge(ring2_used, m + 1)
                    gp, r = divmod(m, GRP)
                    for g2 in range(2):
                        row = (gp * 8 + g2 * 4 + r) * HD
                        sp.dma_start(ring2[g2 * HD:(g2 + 1) * HD, m], nsa_w_out[0, row:row + HD, nh * 512:(nh + 1) * 512]
                                     ).then_inc(ring2_in[m], 16)
                if nh == 0:
                    sp.wait_ge(e_pv, NB)
                    sp.dma_start(gain, ln_g[1:2, :].broadcast_to([P, DM])).then_inc(s_ln, 16)
                    sp.dma_start(offs, ln_b[1:2, :].broadcast_to([P, DM])).then_inc(s_ln, 16)
            for t in range(4):
                sp.wait_ge(ln_done, TT + t + 1)
                sp.dma_start(y_prompt[0, t * P:(t + 1) * P], xr[:, t]).then_inc(s_cpy, 16)
            sp.wait_ge(ln_done, 2 * TT)
            sp.dma_start(y_sample.rearrange("b t m -> (b t) m"), xr[0:64, 4, :]).then_inc(s_cpy, 16)
            sp.wait_ge(s_cpy, 112)

        @block.gpsimd
        def _(pool):
            ch = Chain(pool, pool_s)
            ch.mark(pool.memset(ident, 0.0))
            ch.mark(pool.memset(tri, 0.0))
            ch.mark(pool.memset(quad, 1.0))
            ch.mark(pool.memset(wmask, 0.0))
            ch.mark(pool.memset(cmask, 0.0))
            ch.mark(pool.memset(cvalid, 1.0))
            pool.memset(ones, 1.0).then_inc(s_const, 1)
            ch.link(pool.memset(w2pad[:, 0, HD:P], 0.0))
            pool.memset(w2pad[:, 1, 0:HD], 0.0).then_inc(s_const, 1)

            def keep(v, fill, pattern, base, mult, op=ALU.is_ge):
                return pool.affine_select(out=v, in_=v, compare_op=op, fill=fill, base=base, pattern=pattern,
                                          channel_multiplier=mult)
            keep(ident, 1.0, [[-1, P]], 0, 1, ALU.not_equal).then_inc(s_const, 1)
            keep(tri, NEG, [[-1, P]], 0, 1).then_inc(s_const, 1)
            q4 = quad.rearrange("p (a b) -> p a b", b=4)
            ch.link(keep(q4, 0.0, [[-4, 32], [0, 4]], 0, 1))
            keep(q4, 0.0, [[4, 32], [0, 4]], 3, -1).then_inc(s_const, 1)
            ch.link(keep(wmask, NEG, [[16, WIN + TS]], -1, -1))
            keep(wmask, NEG, [[-16, WIN + TS]], 16 * WIN, 1).then_inc(s_const, 1)
            keep(cmask, NEG, [[P, 4], [-STR, PC]], -(2 * STR - 1), 1).then_inc(s_const, 1)
            keep(cvalid, 0.0, [[P, 4]], -(2 * STR - 1), 1).then_inc(s_const, 1)

            for c in range(CT):
                pool.wait_ge(yn_act, c + 1)
                pool.tensor_tensor(y[:, c], y[:, c], sz[:, c], ALU.mult).then_inc(yn_ready, 1)

            pool.wait_ge(hp_ev, 2)
            pool.memset(vbd, 0.0).then_inc(vbd_zero, 1)
            pool.wait_ge(q_ev_a, 4 + 8)
            pool.wait_ge(q_ev_v, 4 + 8)
            ch.link(pool.memset(qbd, 0.0))
            for m in range(8):
                gp, r = divmod(m, GRP)
                for g2 in range(2):
                    h = slice(g2 * HD, (g2 + 1) * HD)
                    dst = qbd[h].rearrange("p b a (q g r) -> p b a q g r", q=TS, g=NKV)[:, :, gp, :, gp * 2 + g2, r]
                    pool.tensor_copy(dst, qT[h, m, TP:TOK].rearrange("p (b q) -> p b q", b=NB)).then_inc(qbd_ready, 1)
            pool.wait_ge(qbd_ready, 16)
            pool.wait_ge(g_ev, TT)
            for c in range(2):
                for g2 in range(2):
                    ch.mark(pool.memset(qs[c][(1 - g2) * HD:(2 - g2) * HD, g2], 0.0))
            pool.wait_ge(pool_s, ch.base + ch.n)
            for gp in range(2):
                with pool.Fori(0, 2) as it:
                    for c in range(2):
                        blk = it * 2 + (gp * 4 + c)
                        pool.wait_ge(u_sc, blk * 16 + 16)
                        for g2 in range(2):
                            h = slice(g2 * HD, (g2 + 1) * HD)
                            pool.tensor_copy(qs[c][h, g2], qT[h, bass.ds(blk, 1), 0:TP].rearrange("p m t -> p (m t)")
                                             ).then_inc(qs_ready, 1)

            pool.wait_ge(oT_ps, 4)
            pool.wait_ge(qs_ready, 16)

            def stage_queries(b, c):
                if type(b) is not int or b >= 2:
                    pool.wait_ge(e_s, b * 5 - 5)
                pool.tensor_copy(qb[:, c].rearrange("p g n -> p (g n)"), qbd[:, bass.ds(b, 1)].rearrange("p b g n -> p (b g n)")
                                 ).then_inc(q_stage, 1)

            def stage_values(b, c):
                if type(b) is not int or b >= 2:
                    pool.wait_ge(e_pv, b - 1)
                pool.tensor_copy(vcb[0:NC, c], vc[0:NC, bass.ds(b, 1)].rearrange("p b n -> p (b n)")).then_inc(c_stage, 1)

            staging_order(pool, stage_queries, stage_values)

        @block.scalar
        def _(act):
            for t in range(TT):
                transposed_copy(act, t, 1, s_xps, s_xev, xT)
            act.wait_ge(s_aps, 1)
            act.copy(pars[:, 0:8].rearrange("p c n -> p (c n)"), bank[4][:, 0:8 * NPAR]).then_inc(s_aev, 1)
            act.sem_inc(h_silu, 2)
            act.sem_inc(vc_ev, 1)
            act.sem_inc(gl_free, 1)
            act.sem_inc(st_up, 1)
            act.sem_inc(uo_ready, 1)
            act.sem_inc(state_out[0], 32)
            act.sem_inc(state_out[1], 32)
            act.wait_ge(s_cb, 1)
            with act.Fori(0, NB // 2) as it:
                for c in range(2):
                    b = it * 2 + c

                    def silu(s):
                        act.wait_ge(xt_used, b * 16 + 8 * s + 12)
                        act.wait_ge((kc_ps, vc_ps)[s], b + 1)
                        act.activation(hT[:, s, 0:4 * NC].rearrange("p (g n) -> p g n", g=4),
                                       bank[4 + s][:, :].rearrange("p (g n) -> p g n", g=4)[:, :, 0:NC],
                                       ACT.Silu, bias=cb[:, s:s + 1]).then_inc(h_silu, 1)

                    for n in range(SP2):
                        k = 2 * n + 1
                        act.wait_ge(xp_ready, b * 16 + k + 1)
                        act.wait_ge(xt_used, b * 16 + k + 1)
                        act.copy(xtr[:, k % 4], bank[k % 4][:, :]).then_inc(xt_a, 1)
                        if n == 4:
                            silu(0)
                    silu(1)
                    act.wait_ge(vc_ps, b + 2)
                    act.copy(vc[0:NC, bass.ds(b, 1), :].rearrange("p b v -> p (b v)"), bank[7][0:NC, 0:256]).then_inc(vc_ev, 1)

            with act.Fori(0, CT // 2) as it:
                for c in range(2):
                    ct = it * 2 + c
                    act.wait_ge(conv_done, ct + 1)
                    act.copy(par[:, c], pars[:, bass.ds(ct, 1), :].rearrange("p c n -> p (c n)")).then_inc(par_ready, 1)
                    act.wait_ge(par_ready, ct + 1)
                    p0 = 2 * (c * 3 % 2)
                    act.wait_ge(gl_ps, ct + 1)
                    act.wait_ge(a_free, ct + 1)
                    for h in range(2):
                        last = act.activation(sgl[:, h * HALF:(h + 1) * HALF], bank[p0 + h][:, 0:HALF], ACT.Sigmoid,
                                              bias=par[:, c, TAPS + 1:TAPS + 2])
                    last.then_inc(gl_free, 1)
                    act.wait_ge(st_ps, ct + 1)
                    act.copy(ups[c][:, :, 0:TAPS - 1], bank[4][:, 0:NB * (TAPS - 1)].rearrange("p (b n) -> p b n", b=NB)
                             ).then_inc(st_up, 1)
                    act.wait_ge(a_free, ct + 2)
                    act.copy(ups[c][:, :, TAPS - 1:], usc[:, c].rearrange("p (b n) -> p b n", b=NB)).then_inc(st_up, 1)
                    act.wait_ge(z_ps, ct + 1)
                    act.wait_ge(z_free, ct + 1)
                    for h in range(2):
                        last = act.activation(sgz[:, h * HALF:(h + 1) * HALF], bank[p0 + h][:, 0:HALF], ACT.Sigmoid,
                                              bias=par[:, c, TAPS + 2:TAPS + 3])
                    last.then_inc(sgz_ready, 1)
                    act.wait_ge(u_ps, ct + 1)
                    act.wait_ge(state_out[c], it * 32 + 32)
                    act.copy(uo[0:30, c, 0:P], bank[5][0:30, 0:P])
                    act.copy(uo[0:64, c, P:256], bank[5][0:64, P:256]).then_inc(uo_ready, 1)
                    col = it * 256 + c * P
                    act.wait_ge(uo_ready, ct + 2)
                    act.dma_start(state_p[0, 0, :, bass.ds(col, P)], uo[0:30, c, 0:P]).then_inc(state_out[c], 16)
                    act.dma_start(state_s[0, :, TAPS - 1 - TS:TAPS - 1, bass.ds(col, P)], uo[0:64, c, P:256]
                                  ).then_inc(state_out[c], 16)

            for c in range(2):
                act.wait_ge(state_out[c], 16 * CT + 32)
            act.wait_ge(a_free, CT + 1)
            act.wait_ge(z_free, CT + 1)
            for c in range(CT):
                act.wait_ge(conv_done, c + 3)
                if c >= 2:
                    act.wait_ge(sq_used, c - 1)
                act.activation(sq[c % 2], y[:, c], ACT.Square).then_inc(sq_ready, 1)
            act.wait_ge(var_ready, 1)
            act.activation(acc, acc, ACT.Sqrt).then_inc(std_ready, 1)
            for c in range(CT):
                act.wait_ge(norm_done, c + 1)
                act.activation(y[:, c], y[:, c], ACT.Silu, bias=pars[:, c, TAPS + 5:TAPS + 6],
                               scale=pars[:, c, TAPS + 4:TAPS + 5]).then_inc(yn_act, 1)
            deviations(act, 2)

            for t in range(TT):
                transposed_copy(act, t, 1, x1_ps, x1_ev, xT)
            act.sem_inc(q_ev_a, 4)
            act.wait_ge(kv_ev, 3 * TT + 5)
            act.dma_start(kv_p[0, 0].rearrange("(t p) s g d -> p t (s g d)", p=P), kvr[:, 0:4, 0:1024]).then_inc(kv_out, 16)
            act.dma_start(kv_s[0].rearrange("b t s g d -> (b t) (s g d)"), kvr[0:64, 4, 0:1024]).then_inc(kv_out, 16)
            act.dma_start(win_p[0, 0].rearrange("(t p) s g d -> p t (s g d)", p=P), kvr[:, 0:4, 1024:1536]).then_inc(kv_out, 16)
            act.dma_start(win_s[0, :, WIN - TS:WIN].rearrange("b t s g d -> b t (s g d)"), kvr[0:64, 4, 1024:1536]
                          ).then_inc(kv_out, 16)
            with act.Fori(0, 2) as it:
                for r in range(GRP):
                    act.wait_ge(q_ps, it * 7 + (2 * r + 1))
                    act.mul(qT[:, bass.ds(it * 4 + r, 1), 0:HALF].rearrange("p m t -> p (m t)"), bank[2 * r][:, 0:HALF],
                            HD ** -0.5).then_inc(q_ev_a, 1)
            with act.Fori(0, 2) as it:
                for t in range(TT):
                    n = ROWS[t]
                    if t < TT - 1:
                        act.wait_ge(zz_ps, it * 4 + (t + 1))
                    else:
                        act.wait_ge(ring_used, it * RING + (2 * CT + 6 * RING))
                    act.wait_ge(zz_ev, it * 5 + (t + 4 + (t == 0)))
                    act.activation(sig[0:n, t % 2], bank[t][0:n, :], ACT.Sigmoid).then_inc(zz_sg, 1)
            for t in range(TT):
                n = ROWS[t]
                if t < TT - 1:
                    act.wait_ge(g_ps, t + 1)
                else:
                    act.wait_ge(ring_used, 2 * CT + 8 * RING)
                act.activation(gates[0:n, t].rearrange("p h j -> p (h j)"), bank[t][0:n, 0:48], ACT.Sigmoid).then_inc(g_ev, 1)
            for n in (1, 3):
                act.wait_ge(kt_ps, n + 1)
                act.copy(ktp[:, n // 2, n % 2], bank[4 + n][:, :]).then_inc(kt_ev_a, 1)
            act.wait_ge(kt_ps, 6)
            act.copy(zts.rearrange("p m n -> p (m n)"), bank[1][:, :]).then_inc(kt_ev_a, 1)
            for n in (1, 3):
                act.wait_ge(xtp_ps, n + 1)
                act.copy(xtp[:, 4 * n:4 * n + 4].rearrange("p k g n -> p (k g n)"), bank[4 + n][:, :]).then_inc(xtp_ev_a, 1)
            for st_ in range(2):
                act.wait_ge(hp_ps, st_ + 1)
                act.activation(htp[:, st_, 0:4 * PCN], bank[2 + st_][:, 0:4 * PCN], ACT.Silu, bias=cb[:, st_:st_ + 1]
                               ).then_inc(hp_ev, 1)
            for i in range(4):
                act.wait_ge(cs_mx, i + 1)
                act.activation(pc, pc, ACT.Exp).then_inc(cs_ex, 1)
                act.wait_ge(ct_ps, i + 1)
                if i:
                    act.wait_ge(co_ps, i)
                act.copy(pcT, bank[4 + i % 2][:, :]).then_inc(ct_ev, 1)
            for gp in range(2):
                with act.Fori(0, 2) as it:
                    g0 = it * 32 + gp * 64
                    for u in range(33):
                        if u < 32:
                            n = (UNITS[u][1] + 1) * P
                            act.wait_ge(u_mx, g0 + (u + 1))
                            if u >= 3:
                                act.wait_ge(u_tp, g0 + (u - 2))
                            act.activation(prob[:, u % 3, 0:n], bank[u % 3][:, 0:n], ACT.Exp, bias=ust[:, u % 4:u % 4 + 1],
                                           accum_out=ust[:, 4 + u % 4:5 + u % 4]).then_inc(u_ex, 1)
                        if u >= 1:
                            v = u - 1
                            n = (UNITS[v][1] + 1) * P
                            act.wait_ge(u_tp, g0 + u)
                            if v >= 2:
                                act.wait_ge(u_pv, g0 + (v - 1))
                            act.copy(probT[:, v % 2, 0:n], bank[3 + v % 2][:, 0:n]).then_inc(u_pt, 1)
            for t in range(4):
                transposed_copy(act, t, 1, oT_ps, oT_ev, oT)

            def first(b, c):
                act.wait_ge(e_cm, b + 2)
                act.activation(pcn, bank[0][:, 0:NC], ACT.Exp, bias=sst[:, 0:1], accum_out=sst[:, 1:2]).then_inc(e_cx, 1)
                for n in range(5):
                    act.wait_ge(e_tp, b * 5 + (n + 1))
                    if n >= 2:
                        act.wait_ge(e_s, b * 5 + (n - 1))
                    for g in range(2):
                        act.copy(ktb[n % 2][:, g], bank[3 + g][:, :]).then_inc(e_te, 1)

            def soften(b, c):
                def exponentials(n):
                    act.wait_ge(e_nm, b * 2 + (n + 1))
                    v = pb[c][:, 2056:2576] if n == 0 else pb[c][:, 0:2056]
                    act.activation(v, v, ACT.Exp, bias=sst[:, 8 + n:9 + n], accum_out=sst[:, 10 + n:11 + n]).then_inc(e_ex, 1)
                return [lambda: exponentials(0), lambda: exponentials(1)]

            def second(b, c, soft):
                for n in (1, 3, 5):
                    act.wait_ge(e_pp, b * 7 + (n + 1))
                    if n == 1:
                        act.copy(pt[0:TS, n % 4, 0:P], bank[4][0:TS, 0:P])
                        act.copy(pt[0:NC, n % 4, P:2 * P], bank[4][0:NC, P:2 * P]).then_inc(e_pt_a, 1)
                        for step in soft:
                            step()
                    else:
                        act.copy(pt[:, n % 4], bank[4][:, :]).then_inc(e_pt_a, 1)

            sample_order(act, first, soften, second)
            deviations(act, 3)


        @block.vector
        def _(dve):
            ch = Chain(dve, dve_s)
            for t in range(TT):
                transposed_copy(dve, t, 0, s_xps, s_xev, xT)
            dve.wait_ge(s_aps, 1)
            ch.mark(dve.tensor_copy(pars[:, 8:16].rearrange("p c n -> p (c n)"), bank[5][:, 0:8 * NPAR]))
            dve.tensor_copy(auxT, bank[6][:, 0:34]).then_inc(s_aev, 1)
            dve.wait_ge(s_cbp, 1)
            dve.wait_ge(s_aev, 2)
            dve.tensor_tensor(cb, bank[7][:, 0:2], auxT[:, 32:34], ALU.add).then_inc(s_cb, 1)
            dve.sem_inc(xt_used, 4)
            dve.sem_inc(kc_ev, 1)
            dve.sem_inc(a_free, 1)
            dve.sem_inc(z_free, 1)
            dve.sem_inc(conv_done, 2)

            def regroup(b, c, s):
                dve.tensor_copy(rl[:, s].rearrange("p g q n -> p g (q n)").rearrange("p g (t d) -> p g t d", d=HD),
                                xc[:, c].rearrange("p t (s g d) -> p s g t d", s=2, g=NKV)[:, s]).then_inc(rl_ready, 1)

            dve.wait_ge(s_aps, 1)
            dve.wait_ge(xc_in[0], 256)
            for s in range(2):
                regroup(0, 0, s)

            def compress_copies(it, last):
                for c in range(2):
                    b = it * 2 + c
                    for n in range(SP2):
                        k = 2 * n
                        dve.wait_ge(xp_ready, b * 16 + k + 1)
                        dve.wait_ge(xt_used, b * 16 + k + 1)
                        dve.tensor_copy(xtr[:, k % 4], bank[k % 4][:, :]).then_inc(xt_v, 1)
                        if n in (4, 7) and not (last and c):
                            if n == 4:
                                dve.wait_ge(xc_in[1 - c], (it + c) * 256 + 256)
                            s = n // 7
                            dve.wait_ge(xp_ready, b * 16 + 8 * s + 8)
                            regroup(b + 1, 1 - c, s)
                    dve.wait_ge(kc_ps, b + 2)
                    dve.tensor_copy(kcT[:, bass.ds(b, 1)].rearrange("p b g n -> p (b g n)"), bank[6][:, 0:2 * NC]
                                    ).then_inc(kc_ev, 1)

            with dve.Fori(0, NB // 2 - 1) as it:
                compress_copies(it, False)
            compress_copies(NB // 2 - 1, True)

            for c in range(2):
                ch.mark(dve.memset(upp[c][:, 0:CONV_AHEAD], 0.0))
            setup = ch.n
            dve.wait_ge(dve_s, setup)
            PER = 2 * (TAPS - 1)
            with dve.Fori(0, CT // 2) as it:
                for c in range(2):
                    ct = it * 2 + c
                    ch.enter(setup + ct * PER)
                    pa, pz = 2 * ((c * 3 + 1) % 2), 2 * ((c * 3 + 2) % 2)
                    ba, bz, bw = (par[:, c, n:n + 1] for n in (TAPS, TAPS + 2, TAPS + 3))
                    dve.wait_ge(par_ready, ct + 1)
                    dve.wait_ge(a_ps, ct + 1)
                    dve.wait_ge(gl_free, ct + 2)
                    rest = TP - HALF
                    dve.scalar_tensor_tensor(upp[c][:, CONV_AHEAD:CONV_AHEAD + HALF], bank[pa][:, 0:HALF], ba,
                                             sgl[:, 0:HALF], ALU.add, ALU.mult)
                    dve.scalar_tensor_tensor(upp[c][:, CONV_AHEAD + HALF:], bank[pa + 1][:, 0:rest], ba,
                                             sgl[:, HALF:TP], ALU.add, ALU.mult)
                    dve.scalar_tensor_tensor(
                        usc[:, c], bank[pa + 1][:, rest:HALF], ba, sgl[:, TP:TOK], ALU.add, ALU.mult).then_inc(a_free, 1)
                    dve.wait_ge(a_free, ct + 2)
                    yp, ys = split(acc)
                    ys = ys.rearrange("p (b n) -> p b n", b=NB)
                    op, os_ = split(y[:, bass.ds(ct, 1)].rearrange("p c t -> p (c t)"))
                    os_ = os_.rearrange("p (b n) -> p b n", b=NB)
                    for k in range(TAPS):
                        w = par[:, c, k:k + 1]
                        for grp in range(2):
                            if k == 0 and grp:
                                dve.wait_ge(st_up, 2 * ct + 3)
                            src = upp[c][:, k:k + TP] if grp == 0 else ups[c][:, :, k:k + TS]
                            a0 = (yp, ys)[grp]
                            dst = (op, os_)[grp] if k == TAPS - 1 else a0
                            if k == 0:
                                ch.mark(dve.tensor_scalar(dst, src, w, bw, ALU.mult, ALU.add))
                            else:
                                dve.wait_ge(dve_s, ch.base + ch.n - (k < TAPS - 1 or grp == 0))
                                ins = dve.scalar_tensor_tensor(dst, src, w, a0, ALU.mult, ALU.add)
                                if k < TAPS - 1:
                                    ch.mark(ins)
                                elif grp:
                                    ins.then_inc(conv_done, 1)
                        if k == 14:
                            dve.wait_ge(sgz_ready, ct + 1)
                            for h in range(2):
                                n0 = h * HALF
                                ins = dve.scalar_tensor_tensor(
                                    sz[:, bass.ds(ct, 1), n0:n0 + HALF].rearrange("p c t -> p (c t)"), bank[pz + h][:, 0:HALF], bz,
                                    sgz[:, n0:n0 + HALF], ALU.add, ALU.mult)
                            ins.then_inc(z_free, 1)
                    assert ch.n == PER
            ch.enter(setup + CT * PER)

            mu, rstd, tmp = sgl, acc, sgz
            dve.wait_ge(sq_used, CT)
            dve.wait_ge(conv_done, CT + 2)
            for h in range(2):
                ch.mark(dve.tensor_scalar(mu[:, h * HALF:(h + 1) * HALF], bank[h][:, 0:HALF], 1.0 / DIN, None, ALU.mult))
            dve.wait_ge(dve_s, ch.base + ch.n)
            ch.link(dve.tensor_tensor(tmp, mu, mu, ALU.mult))
            for h in range(2):
                ch.mark(dve.scalar_tensor_tensor(rstd[:, h * HALF:(h + 1) * HALF], bank[2 + h][:, 0:HALF], 1.0 / DIN,
                                                 tmp[:, h * HALF:(h + 1) * HALF], ALU.mult, ALU.subtract))
            dve.wait_ge(dve_s, ch.base + ch.n)
            dve.tensor_scalar(rstd, rstd, EPS, None, ALU.add).then_inc(var_ready, 1)
            dve.wait_ge(std_ready, 1)
            ch.link(dve.reciprocal(rstd, rstd))
            for c in range(CT):
                ch.link(dve.tensor_tensor(y[:, c], y[:, c], mu, ALU.subtract))
                dve.tensor_tensor(y[:, c], y[:, c], rstd, ALU.mult).then_inc(norm_done, 1)

            for nh in range(2):
                for t in range(TT):
                    n = ROWS[t]
                    if t < TT - 1:
                        dve.wait_ge(o_ps, nh * (TT - 1) + t + 1)
                    else:
                        dve.wait_ge(ring_used, (nh + 1) * CT)
                    dve.scalar_tensor_tensor(xr[0:n, t, nh * 512:(nh + 1) * 512], xr[0:n, t, nh * 512:(nh + 1) * 512], ALPHA,
                                             bank[t][0:n, :], ALU.mult, ALU.add).then_inc(o_free, 1)
            layer_norm(dve, ch, 2 * TT, 32, 2)

            for t in range(TT):
                transposed_copy(dve, t, 0, x1_ps, x1_ev, xT)
            dve.sem_inc(kv_ev, 5)
            dve.sem_inc(q_ev_v, 4)
            dve.sem_inc(zz_ev, 5)
            with dve.Fori(0, 3) as it:
                for t in range(TT):
                    n = ROWS[t]
                    if t < TT - 1:
                        dve.wait_ge(kv_ps, it * 4 + (t + 1))
                    else:
                        dve.wait_ge(ring_used, it * RING + (2 * CT + RING))
                    dve.tensor_copy(kvr[0:n, t, bass.ds(it * 512, 512)], bank[t][0:n, :]).then_inc(kv_ev, 1)
            with dve.Fori(0, 2) as it:
                for r in range(GRP):
                    if r < GRP - 1:
                        dve.wait_ge(q_ps, it * 7 + (2 * r + 2))
                    else:
                        dve.wait_ge(ring_used, it * RING + (2 * CT + 4 * RING))
                    dve.tensor_scalar(qT[:, bass.ds(it * 4 + r, 1), HALF:TOK].rearrange("p m t -> p (m t)"),
                                      bank[2 * r + 1][:, 0:HALF], HD ** -0.5, None, ALU.mult).then_inc(q_ev_v, 1)
            with dve.Fori(0, 2) as it:
                for t in range(TT):
                    n = ROWS[t]
                    dve.wait_ge(zz_sg, it * 5 + (t + 1))
                    dve.tensor_tensor(zr[0:n, t, bass.ds(it * 512, 512)], bank[t][0:n, :], sig[0:n, t % 2], ALU.mult
                                      ).then_inc(zz_ev, 1)
            for n in (0, 2):
                dve.wait_ge(kt_ps, n + 1)
                dve.tensor_copy(ktp[:, n // 2, n % 2], bank[4 + n][:, :]).then_inc(kt_ev, 1)
            dve.wait_ge(kt_ps, 5)
            dve.tensor_copy(kts.rearrange("p s g n -> p (s g n)"), bank[0][:, 0:256]).then_inc(kt_ev, 1)
            for n in (0, 2):
                dve.wait_ge(xtp_ps, n + 1)
                dve.tensor_copy(xtp[:, 4 * n:4 * n + 4].rearrange("p k g n -> p (k g n)"), bank[4 + n][:, :]).then_inc(xtp_ev_v, 1)
            ch.link(dve.memset(kctp, 0.0))
            dve.wait_ge(w2p_ps, 1)
            for g2 in range(2):
                h = slice(g2 * HD, (g2 + 1) * HD)
                dve.tensor_copy(kctp[h, :, g2, 0:PCN], bank[0][h, 0:2 * PCN].rearrange("p (g n) -> p g n", g=2)).then_inc(w2p_ev, 1)
            dve.wait_ge(w2p_ps, 2)
            dve.tensor_copy(vcp[0:PCN], bank[1][0:PCN, 0:256]).then_inc(w2p_ev, 1)

            pc3 = pc.rearrange("p (h n) -> p h n", h=NH)
            for i in range(4):
                def each(v):
                    return v.rearrange("p (h o) -> p h o", o=1).broadcast_to([P, NH, PC])
                dve.wait_ge(cs_ps, i + 1)
                if i:
                    dve.wait_ge(ct_ps, i)
                pc5 = pc.rearrange("p (a g r n) -> p a g r n", a=2, g=2, r=GRP)
                for g2 in range(2):
                    for gp in range(2):
                        ch.mark(dve.tensor_tensor(pc5[:, gp, g2], bank[i][:, :].rearrange(
                            "p (a r g n) -> p a g r n", a=2, r=GRP, g=2)[:, gp, g2], cmask[:, i:i + 1, :].broadcast_to([P, GRP, PC]), ALU.add))
                dve.wait_ge(dve_s, ch.base + ch.n)
                ch.link(dve.tensor_reduce(cst[:, 0:16], pc3, AX, ALU.max))
                dve.tensor_tensor(pc3, pc3, each(cst[:, 0:16]), ALU.subtract).then_inc(cs_mx, 1)
                dve.wait_ge(cs_ex, i + 1)
                ch.link(dve.tensor_reduce(cst[:, 16:32], pc3, AX, ALU.add))
                ch.link(dve.reciprocal(cst[:, 32:48], cst[:, 16:32]))
                ch.link(dve.scalar_tensor_tensor(cst[:, 48:64], cst[:, 32:48], cvalid[:, i:i + 1], gates[:, i, :, 0],
                                                 ALU.mult, ALU.mult))
                dve.tensor_tensor(pc3, pc3, each(cst[:, 48:64]), ALU.mult).then_inc(cs_sc, 1)
                for gp in range(2):
                    dve.wait_ge(co_ps, i + 1)
                    dve.tensor_copy(att[:, i, gp * 4:gp * 4 + 4].rearrange("p r g d -> p g r d"),
                                    bank[6 + gp][:, :].rearrange("p (g r d) -> p g r d", g=2, r=GRP)).then_inc(co_ev, 1)

            dve.sem_inc(u_fo, 3)
            dve.wait_ge(co_ev, 8)
            u0 = ch.n + ch.base
            for gp in range(2):
                with dve.Fori(0, 2) as it:
                    ch.enter(it * 96 + (u0 + gp * 192))
                    g0 = it * 32 + gp * 64
                    for u in range(35):
                        fin = u - 3
                        if u < 32:
                            n = (UNITS[u][1] + 1) * P
                            dve.wait_ge(u_sc, g0 + (33 + u))
                            at_tri = ch.mark(dve.tensor_tensor(bank[u % 3][:, n - P:n], bank[u % 3][:, n - P:n], tri, ALU.add))
                        if fin >= 0:
                            dve.wait_ge(u_pv, g0 + (fin + 1))
                            k = fin % 4
                            at_rec = ch.mark(dve.reciprocal(ust[:, 8 + k:9 + k], ust[:, 4 + k:5 + k]))
                        if u < 32:
                            dve.wait_ge(dve_s, at_tri)
                            dve.tensor_reduce(ust[:, u % 4:u % 4 + 1], bank[u % 3][:, 0:n], AX, ALU.max, negate=True
                                              ).then_inc(u_mx, 1)
                        if fin >= 0:
                            c, g2, i, br = UNITS[fin][3], UNITS[fin][0], UNITS[fin][1], UNITS[fin][2]
                            dve.wait_ge(dve_s, at_rec)
                            gcol = (gp * 8 + g2 * 4 + c) * 3 + 1 + br
                            gate = gates[:, i].rearrange("p h j -> p (h j)")[:, bass.ds(it * 6 + gcol, 1)]
                            ch.link(dve.tensor_tensor(ust[:, 12 + k:13 + k], ust[:, 8 + k:9 + k], gate, ALU.mult))
                            o = att[:, i, bass.ds(it * 2 + (gp * 4 + c), 1), g2].rearrange("p m d -> p (m d)")
                            if br:
                                dve.wait_ge(u_fo, g0 + (fin + 3))
                            dve.scalar_tensor_tensor(o, bank[5 + fin % 3][:, 0:HD], ust[:, 12 + k:13 + k], o, ALU.mult, ALU.add
                                                     ).then_inc(u_fo, 1)
                    assert ch.n == 96
            ch.enter(u0 + 384)
            dve.wait_ge(u_fo, 128 + 3)
            for i in range(4):
                row = att[:, i].rearrange("p m g d -> p (m g d)")
                dve.tensor_tensor(row, row, zr[:, i], ALU.mult).then_inc(oz_ready, 1)
            for t in range(4):
                transposed_copy(dve, t, 0, oT_ps, oT_ev, oT)

            score, work, top, top2, pick = sel[:, 0:33], sel[:, 33:66], sel[:, 66:74], sel[:, 74:82], sel[:, 82:115]
            dve.sem_inc(e_cm, 1)
            dve.sem_inc(e_ma, 1)
            dve.sem_inc(e_oz, 1)
            dve.wait_ge(oT_ps, 4)
            dve.wait_ge(gr_in, 16)
            ch.mark(dve.memset(score[:, 0:1], BIG))
            ch.link(dve.memset(score[:, 31:33], BIG))

            def gate(b, j):
                return gs[:, bass.ds(b, 1), j]

            def first(b, c):
                p = pb[c]
                dve.wait_ge(e_sc, b + 1)
                dve.tensor_tensor(p[:, PAST:PAST + TS], bank[0][:, 128:136], wmask[:, WIN:WIN + TS], ALU.add)
                dve.tensor_tensor(p[:, 2056 + WIN:2576], bank[0][:, 136:144], wmask[:, WIN:WIN + TS], ALU.add)
                dve.tensor_reduce(sst[:, 0:1], bank[0][:, 0:NC], AX, ALU.max, negate=True).then_inc(e_cm, 1)
                dve.wait_ge(e_cx, b + 1)
                ch.link(dve.reciprocal(sst[:, 2:3], sst[:, 1:2]))
                dve.tensor_scalar(pcn, pcn, sst[:, 2:3], None, ALU.mult).then_inc(e_cn, 1)
                dve.wait_ge(e_cn, b + 1)
                ch.mark(dve.tensor_scalar(p[:, 2576:2576 + NC], pcn, gate(b, 0), None, ALU.mult))
                dve.wait_ge(e_s, b * 5 + 1)
                dve.tensor_tensor(p[:, 2056:2056 + WIN], bank[1][:, :], wmask[:, 0:WIN], ALU.add).then_inc(e_ma, 1)
                dve.wait_ge(e_q4, b + 1)
                ch.mark(dve.tensor_reduce(work[:, 0:30], bank[0][:, 260:380].rearrange("p (j o) -> p j o", o=4)[:, :, 0:3], AX, ALU.add))
                ch.mark(dve.tensor_copy(pick[:, 0:30], bank[0][:, 259:379:4]))
                ch.link(dve.tensor_copy(q7, bank[0][:, 263:383:4]))
                ch.link(dve.tensor_tensor(pick[:, 0:30], pick[:, 0:30], q7, ALU.add))
                ch.link(dve.scalar_tensor_tensor(score[:, 1:31], pick[:, 0:30], 0.5, work[:, 0:30], ALU.mult, ALU.add))
                for k, ranked in enumerate((lambda: dve.max(top, score), lambda: dve.match_replace(work, top, score, -1.0),
                                            lambda: dve.max(top2, work), lambda: dve.match_replace(pick, top2, work, -1.0))):
                    ch.mark(dve.memset(sst[:, 16 + k:17 + k], 0.0))
                    ch.link(ranked())
                ch.link(dve.tensor_scalar(pick, pick, -1.0, 1.0, ALU.is_equal, ALU.subtract))
                for n in range(1, 5):
                    dve.wait_ge(e_s, b * 5 + (n + 1))
                    k0 = (n - 1) * 512
                    dve.scalar_tensor_tensor(
                        p[:, k0:k0 + 512].rearrange("p (j o) -> p j o", o=BLK),
                        pick[:, (n - 1) * 8:n * 8].rearrange("p (j o) -> p j o", o=1).broadcast_to([P, 8, BLK]), -NEG,
                        s_bank[n][:, :].rearrange("p (j o) -> p j o", o=BLK), ALU.mult, ALU.add).then_inc(e_ma, 1)

            def soften(b, c):
                parts = (pb[c][:, 2056:2576], pb[c][:, 0:2056])

                def maxima():
                    dve.wait_ge(e_ma, b * 5 + 6)
                    for n in range(2):
                        dve.tensor_reduce(sst[:, 8 + n:9 + n], parts[n], AX, ALU.max, negate=True).then_inc(e_nm, 1)

                def scale(n):
                    dve.wait_ge(e_ex, b * 2 + (n + 1))
                    ch.link(dve.reciprocal(sst[:, 12 + n:13 + n], sst[:, 10 + n:11 + n]))
                    ch.link(dve.tensor_tensor(sst[:, 14 + n:15 + n], sst[:, 12 + n:13 + n], gate(b, 2 - n), ALU.mult))
                    dve.tensor_scalar(parts[n], parts[n], sst[:, 14 + n:15 + n], None, ALU.mult).then_inc(e_scl, 1)
                return [maxima, lambda: scale(0), lambda: scale(1)]

            def second(b, c, soft):
                for n in (0, 2, 4, 6):
                    dve.wait_ge(e_pp, b * 7 + (n + 1))
                    if n == 6:
                        dve.tensor_copy(pt[0:TS, n % 4, 0:P], bank[3][0:TS, 0:P]).then_inc(e_pt_v, 1)
                    else:
                        dve.tensor_copy(pt[:, n % 4], bank[3][:, :]).then_inc(e_pt_v, 1)
                    for step in (soft[0:1], soft[1:3])[n // 2] if n < 4 else ():
                        step()
                dve.wait_ge(e_pv, b + 1)
                for gp in range(2):
                    for g2 in range(2):
                        h = slice(g2 * HD, (g2 + 1) * HD)
                        dve.tensor_tensor(
                            oT[h, gp * 4:gp * 4 + 4, bass.ds(b * TS + TP, TS)].rearrange("p r q -> p q r"),
                            bank[5 + gp][h, 0:64].rearrange("p (q g r) -> p q g r", q=TS, g=2)[:, :, g2],
                            zts[h, gp * 4:gp * 4 + 4, bass.ds(b * TS, TS)].rearrange("p r q -> p q r"), ALU.mult
                            ).then_inc(e_oz, 1)

            sample_order(dve, first, soften, second, ch)

            for nh in range(2):
                for t in range(TT):
                    n = ROWS[t]
                    if t < TT - 1:
                        dve.wait_ge(o2_ps, nh * (TT - 1) + t + 1)
                    else:
                        dve.wait_ge(ring2_used, (nh + 1) * 8)
                    dve.scalar_tensor_tensor(xr[0:n, t, nh * 512:(nh + 1) * 512], xr[0:n, t, nh * 512:(nh + 1) * 512], ALPHA,
                                             bank[t][0:n, :], ALU.mult, ALU.add).then_inc(o_free, 1)
            layer_norm(dve, ch, 4 * TT, 64, 3)


        @block.tensor
        def _(pe):
            pe.wait_ge(s_const, 8)
            pe.wait_ge(s_x, 32)
            transpose_tiles(pe, lambda t, k: xr[:, t, k * P:(k + 1) * P], TT, s_xps, s_xev)
            pe.wait_ge(s_small, 160)
            for c in range(CT):
                pe.transpose(bank[4 + c // 8][:, (c % 8) * NPAR:(c % 8 + 1) * NPAR], aux[0:NPAR, c * P:(c + 1) * P],
                             ident[0:NPAR, 0:NPAR])
            pe.transpose(bank[6][:, 0:34], aux2[0:34, :], ident[0:34, 0:34]).then_inc(s_aps, 1)
            pe.wait_ge(s_wc, 32)
            pe.wait_ge(s_aev, 2)
            for s in range(2):
                for n in range(16):
                    last = pe.matmul(bank[7][:, s:s + 1], wc[:, s, n // 8, n % 8], auxT[:, s * 16 + n:s * 16 + n + 1],
                                     start=n == 0, stop=n == 15)
            last.then_inc(s_cbp, 1)
            pe.wait_ge(s_cb, 1)
            for w in range(2):
                pe.wait_ge(s_xev[w], TT)
            pe.sem_inc(kc_ps, 1)
            pe.sem_inc(vc_ps, 1)

            with pe.Fori(0, NB // 2) as it:
                for c in range(2):
                    b = it * 2 + c

                    def turn(k):
                        s, q = divmod(k, SP2)
                        if q == 0:
                            pe.wait_ge(rl_ready, b * 2 + s + 1)
                        for g in range(NKV):
                            last = pe.transpose(bank[k % 4][:, g * P:(g + 1) * P], rl[:, s, g, q], ident)
                        last.then_inc(xp_ready, 1)

                    turn(0)
                    for k in range(16):
                        s, q = divmod(k, SP2)
                        if k < 15:
                            turn(k + 1)
                        if q == 0:
                            pe.wait_ge(h_silu, b * 2 + s + 1)
                        pe.wait_ge((xt_v, xt_a)[k % 2], b * 8 + k // 2 + 1)
                        h = bank[4 + s][:, :].rearrange("p (g n) -> p g n", g=4)[:, :, 0:NC]
                        x4 = xtr[:, k % 4].rearrange("p (g n) -> p g n", g=4)
                        for j in range(2):
                            last = pe.matmul(h, wc[:, s, j, q], x4[:, :, j:j + NC], start=(q == 0 and j == 0),
                                             stop=(q == SP2 - 1 and j == 1))
                        last.then_inc(xt_used, 1)
                    pe.wait_ge(h_silu, b * 2 + 3)
                    pe.wait_ge(kc_ev, b + 1)
                    hk = hT[:, 0, 0:4 * NC].rearrange("p (a g n) -> p a g n", a=2, g=2)
                    for g in range(2):
                        last = pe.matmul(bank[6][:, 0:2 * NC].rearrange("p (a n) -> p a n", a=2), w2pad[:, g], hk[:, :, g],
                                         start=g == 0, stop=g == 1)
                    last.then_inc(kc_ps, 1)
                    pe.wait_ge(h_silu, b * 2 + 4)
                    pe.wait_ge(vc_ev, b + 1)
                    for g in range(NKV):
                        last = pe.matmul(bank[7][0:NC, g * HD:(g + 1) * HD], hT[:, 1, g * NC:(g + 1) * NC], w2v,
                                         start=True, stop=True)
                    last.then_inc(vc_ps, 1)

            pe.wait_ge(vc_ev, NB + 1)
            pe.wait_ge(kc_ev, NB + 1)
            pe.wait_ge(xt_v, NB * 8)
            pe.wait_ge(xt_a, NB * 8)
            with pe.Fori(0, CT // 2) as it:
                for c in range(2):
                    ct = it * 2 + c

                    def product(n, part, ready):
                        p0 = 2 * ((c * 3 + n) % 2)
                        for h in range(2):
                            for k in range(KT):
                                last = pe.matmul(bank[p0 + h][:, 0:HALF], wi[:, c, part, k], xT[:, k, h * HALF:(h + 1) * HALF],
                                                 start=k == 0, stop=k == KT - 1)
                        last.then_inc(ready, 1)

                    pe.wait_ge(wi_in[c], it * 64 + 64)
                    pe.wait_ge(a_free, ct + 1)
                    product(0, 1, gl_ps)
                    pe.wait_ge(st_up, 2 * ct + 1)
                    for h in range(2):
                        last = pe.transpose(bank[4][:, h * 120:(h + 1) * 120], st[0:120, c, h], ident[0:120, 0:120])
                    last.then_inc(st_ps, 1)
                    pe.wait_ge(z_free, ct + 1)
                    product(1, 0, a_ps)
                    pe.wait_ge(gl_free, ct + 2)
                    product(2, 2, z_ps)
                    pe.wait_ge(a_free, ct + 2)
                    pe.wait_ge(uo_ready, ct + 1)
                    pe.transpose(bank[5][0:30, 0:P], upp[c][:, TP:TP + CONV_AHEAD], ident)
                    pe.transpose(bank[5][0:64, P:256], usc[:, c], ident).then_inc(u_ps, 1)

            pe.wait_ge(z_free, CT + 1)
            for c in range(CT):
                pe.wait_ge(conv_done, c + 3)
                pe.wait_ge(sq_ready, c + 1)
                for h in range(2):
                    pe.matmul(bank[h][:, 0:HALF], ones, y[:, c, h * HALF:(h + 1) * HALF], start=c == 0, stop=c == CT - 1)
                    last = pe.matmul(bank[2 + h][:, 0:HALF], ones, sq[c % 2][:, h * HALF:(h + 1) * HALF], start=c == 0,
                                     stop=c == CT - 1)
                last.then_inc(sq_used, 1)

            for nh in range(2):
                for c in range(CT):
                    n = nh * CT + c
                    pe.wait_ge(yn_ready, c + 1)
                    pe.wait_ge(ring_in[n % RING], 16 * (n // RING + 1))
                    for t in range(TT):
                        r = ROWS[t]
                        if nh == 1 and c == 0:
                            pe.wait_ge(o_free, t + 1)
                        last = pe.matmul(bank[t][0:r, :], y[:, c, t * P:t * P + r], ring[:, n % RING], start=c == 0,
                                         stop=c == CT - 1)
                        if t == TT - 1:
                            last.then_inc(ring_used, 1)
                        elif c == CT - 1:
                            last.then_inc(o_ps, 1)

            pe.wait_ge(o_free, 2 * TT)
            transpose_tiles(pe, lambda t, k: xr[:, t, k * P:(k + 1) * P], TT, x1_ps, x1_ev, ln_done)
            for w in range(2):
                pe.wait_ge(x1_ev[w], TT)

            def x_tile(k, t):
                return xT[:, k, t * P:t * P + ROWS[t]]

            with pe.Fori(0, 3) as it:
                for k in range(KT):
                    pe.wait_ge(ring_in[k], it * 16 + 80)
                    token_product(pe, x_tile, k, ring[:, k], 512, k == 0, k == KT - 1,
                                  lambda t: pe.wait_ge(kv_ev, it * 5 + (t + 1)), kv_ps).then_inc(ring_used, 1)
            pe.wait_ge(kv_ev, 20)
            with pe.Fori(0, 2) as it:
                for k in range(KT):
                    pe.wait_ge(ring_in[k], it * 32 + 144)
                    for r in range(GRP):
                        if k == 0:
                            pe.wait_ge(q_ev_a, it * 4 + (r + 1))
                            pe.wait_ge(q_ev_v, it * 4 + (r + 1))
                        for h in range(2):
                            last = pe.matmul(bank[2 * r + h][:, 0:HALF], ring[:, k, r * P:(r + 1) * P],
                                             xT[:, k, h * HALF:(h + 1) * HALF], start=k == 0, stop=k == KT - 1)
                            if r == GRP - 1 and h == 1:
                                last.then_inc(ring_used, 1)
                            elif k == KT - 1:
                                last.then_inc(q_ps, 1)
            pe.wait_ge(q_ev_a, 12)
            pe.wait_ge(q_ev_v, 12)
            with pe.Fori(0, 2) as it:
                for k in range(KT):
                    pe.wait_ge(ring_in[k], it * 32 + 208)
                    token_product(pe, x_tile, k, ring[:, k], 512, k == 0, k == KT - 1,
                                  lambda t: pe.wait_ge(zz_ev, it * 5 + (t + 1)), zz_ps).then_inc(ring_used, 1)
            for k in range(KT):
                pe.wait_ge(ring_in[k], 256)
                token_product(pe, x_tile, k, ring[:, k, 0:48], 48, k == 0, k == KT - 1,
                              lambda t: pe.wait_ge(zz_ev, 11 + t), g_ps).then_inc(ring_used, 1)
            pe.wait_ge(g_ev, TT)
            pe.sem_inc(u_sc, 32)
            for n in range(4):
                for t in range(4):
                    col = (2 + 2 * (n // 2)) * 256 + (n % 2) * P
                    last = pe.transpose(bank[4 + n][:, t * P:(t + 1) * P], kvr[:, t, col:col + P], ident)
                last.then_inc(kt_ps, 1)
            for n in range(4):
                col = (2 + 2 * (n // 2)) * 256 + (n % 2) * P
                last = pe.transpose(bank[0][:, n * 64:(n + 1) * 64], kvr[0:64, 4, col:col + P], ident[0:64, 0:64])
            last.then_inc(kt_ps, 1)
            for m in range(8):
                last = pe.transpose(bank[1][:, m * 64:(m + 1) * 64], zr[0:64, 4, m * P:(m + 1) * P], ident[0:64, 0:64])
            last.then_inc(kt_ps, 1)

            pe.wait_ge(kt_ev, 3)
            pe.wait_ge(kt_ev_a, 3)
            pe.wait_ge(rlp_in, 128)
            for n in range(4):
                for k in range(4 * n, 4 * n + 4):
                    for g in range(NKV):
                        last = pe.transpose(bank[4 + n][:, (k % 4) * P + g * PC:(k % 4) * P + (g + 1) * PC],
                                            rlp[k // 8][0:PC, g, k % 8], ident[0:PC, 0:PC])
                last.then_inc(xtp_ps, 1)
            for k in range(16):
                s, q = divmod(k, SP2)
                if k % 4 == 0:
                    pe.wait_ge((xtp_ev_v, xtp_ev_a)[k // 4 % 2], k // 8 + 1)
                h = bank[2 + s][:, 0:4 * PCN].rearrange("p (g n) -> p g n", g=4)
                for j in range(2):
                    last = pe.matmul(h, wc[:, s, j, q], xtp[:, k, :, j:j + PCN], start=(q == 0 and j == 0),
                                     stop=(q == SP2 - 1 and j == 1))
                if q == SP2 - 1:
                    last.then_inc(hp_ps, 1)
            pe.wait_ge(hp_ev, 1)
            hk = htp[:, 0, 0:4 * PCN].rearrange("p (a g n) -> p a g n", a=2, g=2)
            for g in range(2):
                last = pe.matmul(bank[0][:, 0:2 * PCN].rearrange("p (a n) -> p a n", a=2), w2pad[:, g], hk[:, :, g],
                                 start=g == 0, stop=g == 1)
            last.then_inc(w2p_ps, 1)
            pe.wait_ge(hp_ev, 2)
            for g in range(NKV):
                last = pe.matmul(bank[1][0:PCN, g * HD:(g + 1) * HD], htp[:, 1, g * PCN:(g + 1) * PCN], w2v,
                                 start=True, stop=True)
            last.then_inc(w2p_ps, 1)

            pe.wait_ge(w2p_ev, 3)
            for i in range(4):
                for m in range(8):
                    last = pe.matmul(bank[i][:, m * 2 * PC:(m + 1) * 2 * PC], qT[:, m, i * P:(i + 1) * P],
                                     kctp[:, m // 4].rearrange("p g n -> p (g n)"), start=True, stop=True)
                last.then_inc(cs_ps, 1)
            pe.wait_ge(vbd_in, 64)
            for i in range(4):
                pe.wait_ge(cs_sc, i + 1)
                if i >= 2:
                    pe.wait_ge(ct_ev, i - 1)
                for g in range(NKV):
                    last = pe.transpose(bank[4 + i % 2][:, g * P:(g + 1) * P], pc[:, g * P:(g + 1) * P], ident)
                last.then_inc(ct_ps, 1)
                pe.wait_ge(ct_ev, i + 1)
                if i:
                    pe.wait_ge(co_ev, 2 * i)
                for g in range(NKV):
                    last = pe.matmul(bank[6 + g // 2][:, (g % 2) * 256:(g % 2 + 1) * 256], pcT[:, g * P:(g + 1) * P], vbd[:, g],
                                     start=True, stop=True)
                last.then_inc(co_ps, 1)

            pe.wait_ge(co_ev, 8)
            for gp in range(2):
                with pe.Fori(0, 2) as it:
                    g0 = it * 32 + gp * 64

                    def scores(u):
                        g2, i, br, c = UNITS[u]
                        if u % 16 == 0:
                            pe.wait_ge(qs_ready, it * 4 + (gp * 8 + 2 * c + 2))
                        if u >= 3:
                            pe.wait_ge(u_ex, g0 + (u - 2))
                        n = (i + 1) * P
                        pe.matmul(bank[u % 3][:, 0:n], qs[c][:, g2, i * P:(i + 1) * P], ktp[:, br, gp, 0:n],
                                  start=True, stop=True).then_inc(u_sc, 1)

                    scores(0)
                    scores(1)
                    for u in range(33):
                        if u + 2 < 32:
                            scores(u + 2)
                        if u < 32:
                            i = UNITS[u][1]
                            pe.wait_ge(u_ex, g0 + (u + 1))
                            if u >= 2:
                                pe.wait_ge(u_pt, g0 + (u - 1))
                            for k in range(i + 1):
                                last = pe.transpose(bank[3 + u % 2][:, k * P:(k + 1) * P], prob[:, u % 3, k * P:(k + 1) * P], ident)
                            last.then_inc(u_tp, 1)
                        if u >= 1:
                            v = u - 1
                            g2, i, br, c = UNITS[v]
                            pe.wait_ge(u_pt, g0 + (v + 1))
                            pe.wait_ge(u_fo, g0 + (v + 1))
                            col = (3 + 2 * br) * 256 + (gp * 2 + g2) * HD
                            for k in range(i + 1):
                                last = pe.matmul(bank[5 + v % 3][:, 0:HD], probT[:, v % 2, k * P:(k + 1) * P], kvr[:, k, col:col + HD],
                                                 start=k == 0, stop=k == i)
                            last.then_inc(u_pv, 1)
            transpose_tiles(pe, lambda t, k: att[:, t, k].rearrange("p g d -> p (g d)"), 4, oT_ps, oT_ev, oz_ready)

            for w in range(2):
                pe.wait_ge(oT_ev[w], 4)
            pe.wait_ge(u_fo, 128 + 3)

            def first(b, c):
                pe.wait_ge(q_stage, b + 1)
                pe.wait_ge(e_cm, b + 1)
                for g in range(2):
                    pe.matmul(bank[0][:, 0:NC], qb[:, c, g], kcT[:, bass.ds(b, 1), g].rearrange("p b n -> p (b n)"),
                              start=g == 0, stop=g == 1)
                for br in range(2):
                    for g in range(2):
                        last = pe.matmul(bank[0][:, 128 + 8 * br:136 + 8 * br], qb[:, c, g], kts[:, br, g, bass.ds(b * TS, TS)],
                                         start=g == 0, stop=g == 1)
                last.then_inc(e_sc, 1)

                def turn(n):
                    if n == 0:
                        pe.wait_ge(win_in[c], (b - c) * 8 + 16)
                    if n == 1:
                        pe.wait_ge(kv_in[c], (b - c) * 128 + 256)
                    for g in range(2):
                        if n:
                            pe.wait_ge(e_te, b * 10 + (2 * n - 1 + g))
                        for t in range(4):
                            src = wk[:, c, t] if n == 0 else kv[:, c, (n - 1) * 4 + t]
                            last = pe.transpose(bank[3 + g][:, t * P:(t + 1) * P], src[:, g * P:(g + 1) * P], ident)
                    last.then_inc(e_tp, 1)

                turn(0)
                for n in range(5):
                    if n < 4:
                        turn(n + 1)
                    pe.wait_ge(e_te, b * 10 + (2 * n + 2))
                    pe.wait_ge(e_ma, b * 5 + max(n - 1, 1))
                    for g in range(2):
                        last = pe.matmul(s_bank[n][:, :], qb[:, c, g], ktb[n % 2][:, g], start=g == 0, stop=g == 1)
                    last.then_inc(e_s, 1)
                    if n == 0:
                        pe.wait_ge(e_cn, b + 1)
                        pe.matmul(bank[0][:, 256:256 + NC], quad, pcn, start=True, stop=True).then_inc(e_q4, 1)

            def second(b, c, _):
                p = pb[c]
                pe.wait_ge(c_stage, b + 1)
                pe.wait_ge(v_in[c], (b - c) * 152 + 304)
                groups = ([[(2056 + t * P, P, wk[:, c, t, 256:512]) for t in range(4)],
                           [(2056 + WIN, TS, vn[0:TS, c, 1]), (2576, NC, vcb[0:NC, c])]]
                          + [[((4 * n + t) * P, P, kv[:, c, 4 * n + t, 256:512]) for t in range(4)] for n in range(4)]
                          + [[(PAST, TS, vn[0:TS, c, 0])]])

                def turn(n):
                    if n >= 2:
                        pe.wait_ge((e_pt_v, e_pt_a)[n % 2], b * (4 - n % 2) + n // 2)
                    pe.wait_ge(e_scl, b * 2 + (1 if n < 2 else 2))
                    for t, (col, rows, _) in enumerate(groups[n]):
                        last = pe.transpose(bank[3 + n % 2][0:rows, t * P:(t + 1) * P], p[:, col:col + rows], ident)
                    last.then_inc(e_pp, 1)

                turn(0)
                pe.wait_ge(e_oz, b * 4 + 1)
                for n in range(7):
                    if n < 6:
                        turn(n + 1)
                    pe.wait_ge((e_pt_v, e_pt_a)[n % 2], b * (4 - n % 2) + (n // 2 + 1))
                    for t, (_, rows, v) in enumerate(groups[n]):
                        for g in range(2):
                            rhs = pt[0:rows, n % 4, t * P:(t + 1) * P].rearrange("p (q g m) -> p g q m", q=TS, g=2)[:, g]
                            last = pe.matmul(bank[5 + g][:, 0:64].rearrange("p (q m) -> p q m", q=TS), v[:, g * P:(g + 1) * P], rhs,
                                             start=n == 0 and t == 0, stop=n == 6)
                last.then_inc(e_pv, 1)

            sample_order(pe, first, lambda b, c: [], second)

            pe.wait_ge(e_cm, NB + 1)
            pe.wait_ge(e_ma, 5 * NB + 1)
            pe.wait_ge(e_oz, 4 * NB + 1)
            for nh in range(2):
                for m in range(8):
                    pe.wait_ge(ring2_in[m], 32 * (nh + 1))
                    token_product(pe, lambda k, t: oT[:, k, t * P:t * P + ROWS[t]], m, ring2[:, m], 512, m == 0, m == 7,
                                  lambda t: nh and pe.wait_ge(o_free, 2 * TT + t + 1), o2_ps).then_inc(ring2_used, 1)



_INS = ["x_prompt", "x_sample", "state_conv", "cache_kv", "cache_win", "page_table", "conv_w_in", "conv_b_in", "conv_dw_w",
        "conv_dw_b", "conv_ln_g", "conv_ln_b", "conv_w_out", "nsa_w_in", "cmp_pe", "cmp_w1", "cmp_b1", "cmp_w2", "nsa_w_out",
        "ln_g", "ln_b"]
_OUTS = [(1, 512, 1024), (8, 8, 1024), (1, 1, 30, 2048), (1, 8, 30, 2048), (1, 1, 512, 4, 4, 64), (1, 8, 8, 4, 4, 64),
         (1, 1, 512, 2, 4, 64), (1, 8, 512, 2, 4, 64)]


def kernel(**inputs):
    import numpy as _np
    import concourse.bacc as _bacc
    from concourse import mybir as _mybir
    from concourse.bass_utils import run_bass_kernel_spmd as _run

    nc = _bacc.Bacc("TRN2", target_bir_lowering=False, num_devices=1)
    arrays, args = {}, []
    for name in _INS:
        a = _np.ascontiguousarray(inputs[name])
        arrays[f"in_{name}_dram"] = a
        args.append(nc.dram_tensor(f"in_{name}_dram", a.shape, _mybir.dt.from_np(a.dtype), kind="ExternalInput").ap())
    for i, shape in enumerate(_OUTS):
        args.append(nc.dram_tensor(f"out_{i}_dram", shape, _mybir.dt.float32, kind="ExternalOutput").ap())
    build_program(nc, *args)
    r = _run(nc, [arrays], core_ids=[0])
    return tuple(r.results[0][f"out_{i}_dram"] for i in range(len(_OUTS)))
```

```python
from contextlib import ExitStack

import concourse.bass as bass
from concourse import mybir

F32 = mybir.dt.float32
I32 = mybir.dt.int32
ALU = mybir.AluOpType
ACT = mybir.ActivationFunctionType
AX = mybir.AxisListType.X

P = 128
DM = 1024
KT = DM // P
DIN = 2048
CT = DIN // P
TAPS = 31
TP = 512
NB, TS = 8, 8
TOK = TP + NB * TS
HALF = TOK // 2
TT = 5
ROWS = [P, P, P, P, NB * TS]
HD = 64
NH = 16
NKV = 4
GRP = NH // NKV
PAST = 2048
PAGE = 128
NPG = PAST // PAGE
STR = 16
SP2 = STR // 2
NC = PAST // STR - 1
PC = TP // STR
PCN = PC - 1
NSEL = 33
BLK = 64
WIN = 512
ALPHA = (2 * 2) ** 0.25
EPS = 1e-5
NEG = -1.0e30
BIG = 3.0e38
RING = 8
NPAR = TAPS + 6
UPS = TS + TAPS - 1
CONV_AHEAD = TAPS - 1
GL, A, Z = 0, 2, 6
ARENA = 53056


UNITS = [(g2, i, br, c) for c in range(2) for g2 in range(2) for i in range(TP // P) for br in range(2)]


class Chain:

    def __init__(self, eng, sem):
        self.eng, self.sem, self.base, self.n = eng, sem, 0, 0

    def mark(self, ins):
        ins.then_inc(self.sem, 1)
        self.n += 1
        return self.base + self.n

    def link(self, ins):
        self.eng.wait_ge(self.sem, self.mark(ins))

    def enter(self, base):
        self.base, self.n = base, 0


def build_program(nc, x_prompt, x_sample, state_conv, cache_kv, cache_win, page_table,
                  conv_w_in, conv_b_in, conv_dw_w, conv_dw_b, conv_ln_g, conv_ln_b, conv_w_out,
                  nsa_w_in, cmp_pe, cmp_w1, cmp_b1, cmp_w2, nsa_w_out, ln_g, ln_b,
                  y_prompt, y_sample, state_p, state_s, kv_p, kv_s, win_p, win_s):
    ctx = ExitStack()
    with ctx:
        def sem(name):
            return ctx.enter_context(nc.semaphore(name))

        arena = ctx.enter_context(nc.sbuf_tensor("arena", [P, ARENA], F32))
        pages = ctx.enter_context(nc.sbuf_tensor("pages", [1, NB * NPG], I32))
        bank = [ctx.enter_context(nc.psum_tensor(f"bank{i}", [P, 512], F32)) for i in range(8)]

        def at(kib, n):
            o = int(kib * 256)
            assert o + n <= ARENA
            return arena[:, o:o + n]

        xr = at(0, TT * DM).rearrange("p (t m) -> p t m", t=TT)
        xT = at(20, KT * TOK).rearrange("p (k t) -> p k t", k=KT)
        kcT = at(38, NB * 2 * NC).rearrange("p (b g n) -> p b g n", b=NB, g=2)
        vc = at(46, NB * 256).rearrange("p (b v) -> p b v", b=NB)
        ident = at(54, P)
        tri = at(54.5, P)
        quad = at(55, P)
        wmask = at(55.5, WIN + TS)
        cmask = at(57.75, 4 * PC).rearrange("p (i n) -> p i n", i=4)
        cvalid = at(58.25, 4)
        w2pad = at(58.5, 2 * P).rearrange("p (g m) -> p g m", g=2)
        w2v = at(59.5, HD)
        auxT = at(59.75, 34)
        cb = at(60, 2)
        par = at(60.25, 2 * NPAR).rearrange("p (c n) -> p c n", c=2)
        pars = at(61, CT * NPAR).rearrange("p (c n) -> p c n", c=CT)
        uo = at(63.5, 2 * 256).rearrange("p (c m) -> p c m", c=2)
        stat = at(65.5, 128)
        gain = at(66, DM)
        offs = at(70, DM)
        wc = at(74, 32 * P).rearrange("p (s j q h) -> p s j q h", s=2, j=2, q=SP2)

        xc = at(90, 2 * 8192).rearrange("p (c s f) -> p c s f", c=2, s=STR)
        rl = at(154, 2 * 4096).rearrange("p (s g q n) -> p s g q n", s=2, g=NKV, q=SP2)
        xtr = at(186, 4 * 512).rearrange("p (c n) -> p c n", c=4)
        hT = at(194, 2 * 512).rearrange("p (c n) -> p c n", c=2)
        aux2 = at(199, P)
        ones = at(206.75, P)

        y = at(114, CT * TOK).rearrange("p (c t) -> p c t", c=CT)
        sz = at(150, CT * TOK).rearrange("p (c t) -> p c t", c=CT)
        wi = at(90, 2 * 3 * KT * P).rearrange("p (c a k n) -> p c a k n", c=2, a=3, k=KT)
        wx = at(150, CT * 512).rearrange("p (c n) -> p c n", c=CT)
        ring = at(90, RING * 512).rearrange("p (r n) -> p r n", r=RING)
        aux = at(191, DIN)
        up = at(191, 2 * 880).rearrange("p (c n) -> p c n", c=2)
        upp = [up[:, c, 0:CONV_AHEAD + TP] for c in range(2)]
        ups = [up[:, c, CONV_AHEAD + TP:CONV_AHEAD + TP + NB * UPS].rearrange("p (b n) -> p b n", b=NB)
               for c in range(2)]
        usc = at(65.5, 2 * 64).rearrange("p (c n) -> p c n", c=2)
        sgl = at(198, TOK)
        acc = at(200.25, TOK)
        acc_odd = at(186, TP)
        y_sum = at(54.5, TOK)
        y_sq = at(188, TOK)
        sgz = at(202.5, TOK)
        st = at(204.75, 2 * 2 * P).rearrange("p (c h m) -> p c h m", c=2, h=2)
        terms = at(66, 64 * (TAPS + 1)).rearrange("p (b n k) -> p b n k", b=NB, n=TS)
        square = at(66, TOK)

        qT = at(106, KT * TOK).rearrange("p (m t) -> p m t", m=8)
        kvr = at(124, TT * 1536).rearrange("p (t n) -> p t n", t=TT)
        zr = at(154, TT * DM).rearrange("p (t n) -> p t n", t=TT)
        gates = at(174, TT * 48).rearrange("p (t h j) -> p t h j", t=TT, j=3)
        ktp = at(175, 4 * TP).rearrange("p (s g n) -> p s g n", s=2, g=2)
        sig = at(186, 2 * 512).rearrange("p (c n) -> p c n", c=2)
        kts = at(194, 4 * 64).rearrange("p (s g n) -> p s g n", s=2, g=2)
        zts = at(195, 8 * 64).rearrange("p (m n) -> p m n", m=8)
        qbd = at(197, NB * 256).rearrange("p (b g n) -> p b g n", b=NB, g=2)
        gs = at(205, NB * 3).rearrange("p (b j) -> p b j", b=NB)
        rlp = [at(k, SP2 * P).rearrange("p (q n) -> p q n", q=SP2) for k in (66, 190)]
        xtp = at(197, 16 * P).rearrange("p (k g n) -> p k g n", k=16, g=NKV)
        htp = at(190, 2 * P).rearrange("p (s n) -> p s n", s=2)
        kctp = at(191, 4 * PC).rearrange("p (a g n) -> p a g n", a=2, g=2)
        vcp = at(192, 256)
        vbd = at(66, 4 * 256).rearrange("p (g n) -> p g n", g=NKV)

        att = at(20, 4 * DM).rearrange("p (i m g d) -> p i m g d", i=4, m=8, g=2)
        qs = [at(k, 2 * TP).rearrange("p (g n) -> p g n", g=2) for k in (186, 70)]
        prob = at(74, 3 * 512).rearrange("p (c n) -> p c n", c=3)
        probT = at(80, 2 * 512).rearrange("p (c n) -> p c n", c=2)
        pc = [at(k, 512) for k in (84, 98)]
        pcT = at(86, 512)
        cst = [at(k, 64) for k in (88, 88.25)]
        ust = at(88.5, 64)
        oT = at(106, KT * TOK).rearrange("p (m t) -> p m t", m=8)

        kv = at(124, 2 * 8192).rearrange("p (c n f) -> p c n f", c=2, n=NPG)
        wk = at(90, 2 * 2048).rearrange("p (c n f) -> p c n f", c=2, n=4)
        pb = [at(20, 2703), at(74, 2703)]
        ktb = [at(k, 1024).rearrange("p (g n) -> p g n", g=2) for k in (31, 85)]
        pt = at(66, 4 * 512).rearrange("p (c n) -> p c n", c=4)
        qb = at(35, 2 * 256).rearrange("p (c g n) -> p c g n", c=2, g=2)
        vcb = at(188, 2 * 256).rearrange("p (c n) -> p c n", c=2)
        vn = at(190, 2 * 512).rearrange("p (c s n) -> p c s n", c=2, s=2)
        pcn = at(37, NC)
        sel = at(37.5, 128)
        sst = at(205.25, 64)
        q7 = at(205.5, 30)
        w_o = at(124, 8 * DM).rearrange("p (m n) -> p m n", m=8)
        gate_rows = nc.dram_tensor("gate_rows", (NB * TS, 48), F32, kind="Internal").ap()

        s_bank = [bank[n] for n in (1, 2, 1, 2, 1)]

        def early(n):
            t, stream = divmod(n, 4)
            stream = (0, 1, 2, 4)[stream]
            return kvr[:, t, stream * 256:(stream + 1) * 256]

        def split(v):
            return v[:, 0:TP], v[:, TP:TOK]

        block = ctx.enter_context(nc.Block())

        s_const = sem("s_const")
        s_small = sem("s_small")
        s_x = sem("s_x")
        s_wc = sem("s_wc")
        s_cpy = sem("s_cpy")
        s_xps = sem("s_xps")
        s_xev = [sem(f"s_xev{w}") for w in range(2)]
        s_aps = sem("s_aps")
        s_aev = sem("s_aev")
        s_cbp = sem("s_cbp")
        s_cb = sem("s_cb")
        s_pg = sem("s_pg")
        xc_in = [sem(f"xc_in{c}") for c in range(2)]
        rl_ready = sem("rl_ready")
        xp_ready = sem("xp_ready")
        xt_v = sem("xt_v")
        xt_a = sem("xt_a")
        xt_used = sem("xt_used")
        h_silu = sem("h_silu")
        kc_ps = sem("kc_ps")
        vc_ps = sem("vc_ps")
        kc_ev = sem("kc_ev")
        vc_ev = sem("vc_ev")
        wi_in = [sem(f"wi_in{c}") for c in range(2)]
        gl_ps = sem("gl_ps")
        a_ps = sem("a_ps")
        z_ps = sem("z_ps")
        gl_free = sem("gl_free")
        a_free = sem("a_free")
        z_free = sem("z_free")
        sgz_ready = sem("sgz_ready")
        par_ready = sem("par_ready")
        st_ps = sem("st_ps")
        st_up = sem("st_up")
        u_ps = sem("u_ps")
        uo_ready = sem("uo_ready")
        state_out = [sem(f"state_out{c}") for c in range(2)]
        conv_done = sem("conv_done")
        conv_s = sem("conv_s")
        sums_ready = sem("sums_ready")
        st_sum = sem("st_sum")
        masks_ready = sem("masks_ready")
        var_ready = sem("var_ready")
        std_ready = sem("std_ready")
        norm_done = sem("norm_done")
        yn_act = sem("yn_act")
        yn_ready = sem("yn_ready")
        ring_in = [sem(f"ring_in{r}") for r in range(RING)]
        ring_used = sem("ring_used")
        wx_in = sem("wx_in")
        o_ps = sem("o_ps")
        o_free = sem("o_free")
        s_ln = sem("s_ln")
        kv_ps = sem("kv_ps")
        kv_ev = sem("kv_ev")
        kv_out = sem("kv_out")
        q_ev_a = sem("q_ev_a")
        q_ev_v = sem("q_ev_v")
        q_ps = sem("q_ps")
        zz_ps = sem("zz_ps")
        zz_sg = sem("zz_sg")
        zz_ev = sem("zz_ev")
        g_ps = sem("g_ps")
        g_ev = sem("g_ev")
        gr_out = sem("gr_out")
        gr_in = sem("gr_in")
        kt_ps = sem("kt_ps")
        kt_ev = sem("kt_ev")
        rlp_in = sem("rlp_in")
        xtp_ps = sem("xtp_ps")
        xtp_ev_v = sem("xtp_ev_v")
        xtp_ev_a = sem("xtp_ev_a")
        hp_ps = sem("hp_ps")
        hp_ev = sem("hp_ev")
        w2p_ps = sem("w2p_ps")
        w2p_ev = sem("w2p_ev")
        vbd_zero = sem("vbd_zero")
        vbd_in = sem("vbd_in")
        qbd_ready = sem("qbd_ready")
        cs_ps = sem("cs_ps")
        cs_mx = sem("cs_mx")
        cs_ex = sem("cs_ex")
        cs_sc = sem("cs_sc")
        ct_ps = sem("ct_ps")
        ct_ev = sem("ct_ev")
        co_ps = sem("co_ps")
        co_ev = sem("co_ev")
        u_sc = sem("u_sc")
        u_mx = sem("u_mx")
        u_ex = sem("u_ex")
        u_tp = sem("u_tp")
        u_pt = sem("u_pt")
        u_pv = sem("u_pv")
        u_fo = sem("u_fo")
        qs_ready = sem("qs_ready")
        oz_ready = sem("oz_ready")
        oT_ps = sem("oT_ps")
        e_sc = sem("e_sc")
        e_cm = sem("e_cm")
        e_cx = sem("e_cx")
        e_cn = sem("e_cn")
        e_q4 = sem("e_q4")
        e_tp = sem("e_tp")
        e_te = sem("e_te")
        e_s = sem("e_s")
        e_ma = sem("e_ma")
        e_nm = sem("e_nm")
        e_ex = sem("e_ex")
        e_scl = sem("e_scl")
        e_pp = sem("e_pp")
        e_pt_v = sem("e_pt_v")
        e_pt_a = sem("e_pt_a")
        e_pv = sem("e_pv")
        e_oz = sem("e_oz")
        oT_ev = [sem(f"oT_ev{w}") for w in range(2)]
        x1_ev = [sem(f"x1_ev{w}") for w in range(2)]
        x1_ps = sem("x1_ps")
        win_in = [sem(f"win_in{c}") for c in range(2)]
        kt_ev_a = sem("kt_ev_a")
        kv_in = [sem(f"kv_in{c}") for c in range(2)]
        v_in = [sem(f"v_in{c}") for c in range(2)]
        vp_in = [sem(f"vp_in{c}") for c in range(2)]
        q_stage = sem("q_stage")
        c_stage = sem("c_stage")
        w_o_in = sem("w_o_in")
        o2_ps = sem("o2_ps")
        ln_done = sem("ln_done")
        dve_s = sem("dve_s")
        pool_s = sem("pool_s")

        PAIRS = (0, 2)
        X1_PAIRS = (5,)

        def x_columns(t, k):
            return xr[:, t, k * P:(k + 1) * P]

        def transposed_copy(eng, t, who, ps, ev, dst, pairs=PAIRS):
            n = ROWS[t]
            eng.wait_ge(ps, t + 1)
            src = bank[pairs[t % len(pairs)] + who][:, :].rearrange("p (k n) -> p k n", k=4)[:, :, 0:n]
            (eng.copy if who else eng.tensor_copy)(dst[:, 4 * who:4 * who + 4, t * P:t * P + n], src).then_inc(ev[who], 1)

        def transpose_tile(pe, src, t, pairs, ps, ev, ready=None):
            n = ROWS[t]
            if ready is not None:
                pe.wait_ge(ready, t + 1)
            for k in range(KT):
                if t >= len(pairs) and k % 4 == 0:
                    pe.wait_ge(ev[k // 4], t - len(pairs) + 1)
                last = pe.transpose(bank[pairs[t % len(pairs)] + k // 4][:, (k % 4) * P:(k % 4) * P + n], src(t, k)[0:n],
                                    ident[0:n, 0:n])
            last.then_inc(ps, 1)

        def token_product(pe, lhs, k, slot, width, first, last_k, free, ready):
            for t in range(TT):
                r = ROWS[t]
                if first:
                    free(t)
                ins = pe.matmul(bank[t][0:r, 0:width], lhs(k, t), slot, start=first, stop=last_k)
                if last_k and t < TT - 1:
                    ins.then_inc(ready, 1)
            return ins

        def sample_order(eng, step, ch=None):
            c0 = (ch.base + ch.n) if ch else 0
            step(0, 0, output=False)
            first = (ch.base + ch.n - c0) if ch else 0
            per = first + (5 if ch else 0)
            with eng.Fori(0, NB // 2 - 1) as it:
                for c in (1, 0):
                    if ch:
                        ch.enter(it * (2 * per) + (c0 + first + (0 if c else per)))
                    step(it * 2 + (1 if c else 2), c)
                    assert not ch or ch.n == per
            if ch:
                ch.enter(c0 + first + (NB - 2) * per)
            step(NB - 1, 1)
            step(NB, 0, scores=False)

        def staging_order(eng, keys, values):
            keys(0, 0)
            keys(1, 1)
            values(0, 0)
            values(1, 1)
            keys(2, 0)
            with eng.Fori(1, NB // 2 - 1) as it:
                keys(it * 2 + 1, 1)
                values(it * 2, 0)
                keys(it * 2 + 2, 0)
                values(it * 2 + 1, 1)
            keys(NB - 1, 1)
            values(NB - 2, 0)
            values(NB - 1, 1)

        def residual(dve, ch, t, nh, product, freed):
            n = ROWS[t]
            half = xr[0:n, t, nh * 512:(nh + 1) * 512]
            dve.scalar_tensor_tensor(half, half, ALPHA, product[0:n, :], ALU.mult, ALU.add).then_inc(o_free, 1)
            dve.wait_ge(o_free, freed)
            ch.mark(dve.bn_stats(stat[0:n, 12 * t + 6 * nh:12 * t + 6 * nh + 6], half))

        def normalise(dve, ch, t, loaded, count):
            n = ROWS[t]
            row = xr[0:n, t]
            dve.wait_ge(dve_s, ch.base + ch.n)
            ch.link(dve.bn_aggr(stat[0:n, 64 + 2 * t:66 + 2 * t], stat[0:n, 12 * t:12 * t + 12].rearrange("p (c s) -> p c s", c=2)))
            dve.tensor_scalar(stat[0:n, 80 + t:81 + t], stat[0:n, 65 + 2 * t:66 + 2 * t], EPS, None, ALU.add).then_inc(var_ready, 1)
            dve.wait_ge(std_ready, count + t)
            ch.link(dve.reciprocal(stat[0:n, 96 + t:97 + t], stat[0:n, 88 + t:89 + t]))
            ch.link(dve.tensor_scalar(row, row, stat[0:n, 64 + 2 * t:65 + 2 * t], stat[0:n, 96 + t:97 + t], ALU.subtract, ALU.mult))
            dve.wait_ge(s_ln, loaded)
            ch.link(dve.tensor_tensor(row, row, gain[0:n], ALU.mult))
            dve.tensor_tensor(row, row, offs[0:n], ALU.add).then_inc(ln_done, 1)

        def deviation(act, t, count):
            n = ROWS[t]
            act.wait_ge(var_ready, count + t)
            act.activation(stat[0:n, 88 + t:89 + t], stat[0:n, 80 + t:81 + t], ACT.Sqrt).then_inc(std_ready, 1)

        @block.sync
        def _(sp):
            sp.dma_start(xr[:, 0:4, :], x_prompt[0].rearrange("(t p) m -> p t m", p=P)).then_inc(s_x, 16)
            sp.dma_start(xr[0:64, 4, :], x_sample.rearrange("b t m -> (b t) m")).then_inc(s_x, 16)
            sp.dma_start(pages[:, :], page_table.rearrange("(o b) n -> o (b n)", o=1)).then_inc(s_pg, 16)
            sp.dma_start(aux2[0:32, :], cmp_pe[0].rearrange("s (q e) d -> (s q) (e d)", e=2)).then_inc(s_small, 16)
            sp.dma_start(aux2[32:34, :], cmp_b1[0]).then_inc(s_small, 16)
            for g in range(2):
                sp.dma_start(w2pad[:, g, g * HD:(g + 1) * HD], cmp_w2[0, 0]).then_inc(s_small, 16)
            sp.dma_start(w2v, cmp_w2[0, 1]).then_inc(s_small, 16)
            sp.dma_start(aux[0:TAPS, :], conv_dw_w[0]).then_inc(s_small, 16)
            sp.dma_start(aux[TAPS:TAPS + 3, :], conv_b_in[0].rearrange("(a n) -> a n", a=3)).then_inc(s_small, 16)
            for r, v in enumerate((conv_dw_b, conv_ln_g, conv_ln_b)):
                sp.dma_start(aux[TAPS + 3 + r:TAPS + 4 + r, :], v).then_inc(s_small, 16)
            for s in range(2):
                sp.dma_start(wc[:, s].rearrange("p j q h -> p (j q) h"),
                             cmp_w1[0, s].rearrange("(q e) d h -> (e d) q h", e=2)).then_inc(s_wc, 16)

            def load_chunks(it):
                for c in range(2):
                    for n in range(NPG):
                        pg = sp.value_load(pages[0:1, bass.ds((it * 2 + c) * NPG + n, 1)], min_val=0, max_val=cache_kv.shape[1] - 1)
                        if n == 0 and type(it) is not int:
                            sp.wait_ge(rl_ready, it * 4 + c * 2 - 2)
                        sp.dma_start(xc[n * 8:n * 8 + 8, c],
                                     cache_kv[0, bass.ds(pg, 1)].rearrange("o (c s) k g d -> (o c) s (k g d)", s=STR)[:, :, 0:512]
                                     ).then_inc(xc_in[c], 16)

            def load_mixer(it):
                for c in range(2):
                    for a in range(3):
                        if a == 0 and type(it) is not int:
                            sp.wait_ge(z_ps, it * 2 + c - 1)
                        sp.dma_start(wi[:, c, a],
                                     conv_w_in[0].rearrange("(k p) n -> p k n", p=P)[:, :, bass.ds(it * 256 + (a * DIN + c * P), P)]
                                     ).then_inc(wi_in[c], 16)
                    sp.dma_start(st[0:120, c],
                                 state_conv[0].rearrange("(h b) t n -> (b t) h n", h=2)[:, :, bass.ds(it * 256 + c * P, P)]
                                 ).then_inc(wi_in[c], 16)

            sp.wait_ge(s_pg, 16)
            load_chunks(0)
            with sp.Fori(1, NB // 2) as it:
                load_chunks(it)
            sp.wait_ge(rl_ready, 2 * NB)
            load_mixer(0)
            with sp.Fori(1, CT // 2) as it:
                load_mixer(it)
            sp.dma_start(state_s[0, :, 0:TAPS - 1 - TS].rearrange("b t n -> b (t n)"),
                         state_conv[0, :, TS:TAPS - 1].rearrange("b t n -> b (t n)")).then_inc(s_cpy, 16)
            sp.dma_start(win_s[0, :, 0:WIN - TS].rearrange("b t k g d -> b (t k g d)"),
                         cache_win[0, :, TS:WIN].rearrange("b t k g d -> b (t k g d)")).then_inc(s_cpy, 16)
            sp.wait_ge(z_ps, CT)
            for c in range(CT):
                if c >= RING:
                    sp.wait_ge(ring_used, c - RING + 1)
                sp.dma_start(ring[:, c % RING], conv_w_out[0, c * P:(c + 1) * P, 0:512]).then_inc(ring_in[c % RING], 16)
            sp.wait_ge(yn_ready, CT)
            sp.dma_start(wx, conv_w_out[0, :, 512:1024].rearrange("(c p) n -> p c n", p=P)).then_inc(wx_in, 16)
            sp.wait_ge(conv_s, CT + 2)
            sp.dma_start(gain, ln_g[0:1, :].broadcast_to([P, DM])).then_inc(s_ln, 16)
            sp.dma_start(offs, ln_b[0:1, :].broadcast_to([P, DM])).then_inc(s_ln, 16)
            w_in = nsa_w_in[0]
            used = CT - RING
            with sp.Fori(0, 3) as it:
                for k in range(KT):
                    sp.wait_ge(ring_used, it * RING + (used + k + 1))
                    sp.dma_start(ring[:, k], w_in[k * P:(k + 1) * P, bass.ds(it * 512 + DM, 512)]).then_inc(ring_in[k], 16)

            def load_permuted(base, used):
                with sp.Fori(0, 2) as it:
                    for k in range(KT):
                        sp.wait_ge(ring_used, it * RING + (used + k + 1))
                        for g in range(2):
                            sp.dma_start(ring[:, k].rearrange("p (r g d) -> p g r d", r=GRP, g=2)[:, g],
                                         w_in[k * P:(k + 1) * P, bass.ds(it * 512 + (base + g * 256), 256)].rearrange(
                                             "p (r d) -> p r d", r=GRP)).then_inc(ring_in[k], 16)
            load_permuted(0, used + 24)
            sp.wait_ge(kv_out, 64)
            for st_ in range(2):
                for g in range(NKV):
                    sp.dma_start(rlp[st_][g * PC:(g + 1) * PC].rearrange("p q (e d) -> p (q e) d", e=2),
                                 kv_p[0, 0, :, st_, g].rearrange("(c t) d -> c t d", t=STR)).then_inc(rlp_in, 16)
            load_permuted(2608, used + 40)
            for k in range(KT):
                sp.wait_ge(ring_used, used + 56 + k + 1)
                sp.dma_start(ring[:, k, 0:48], w_in[k * P:(k + 1) * P, 2560:2608]).then_inc(ring_in[k], 16)
            sp.wait_ge(g_ev, TT)
            sp.dma_start(gate_rows, gates[0:64, 4].rearrange("p h j -> p (h j)")).then_inc(gr_out, 16)
            sp.wait_ge(gr_out, 16)
            sp.dma_start(gs, gate_rows.rearrange("(b q) (h j) -> (q h) b j", b=NB, j=3)).then_inc(gr_in, 16)
            sp.wait_ge(w2p_ev, 3)
            sp.wait_ge(vbd_zero, 1)
            for r in range(GRP):
                sp.dma_start(vbd[32 * r:32 * r + PCN, :, r * HD:(r + 1) * HD], vcp[0:PCN].rearrange("p (g d) -> p g d", g=NKV)
                             ).then_inc(vbd_in, 16)
            def window_keys(b, c):
                sp.dma_start(wk[:, c, :, 0:256], cache_win[0, bass.ds(b, 1), :, 0].rearrange("o (n p) g d -> p (o n) (g d)", p=P)
                             ).then_inc(win_in[c], 16)

            def window_values(b, c):
                sp.dma_start(wk[:, c, :, 256:512], cache_win[0, bass.ds(b, 1), :, 1].rearrange("o (n p) g d -> p (o n) (g d)", p=P)
                             ).then_inc(v_in[c], 16)
                sp.dma_start(vn[0:TS, c, 0], kv_s[0, bass.ds(b, 1), :, 3].rearrange("o t g d -> (o t) (g d)")).then_inc(v_in[c], 16)
                sp.dma_start(vn[0:TS, c, 1], win_s[0, bass.ds(b, 1), WIN - TS:WIN, 1].rearrange("o t g d -> (o t) (g d)")
                             ).then_inc(v_in[c], 16)

            def load_pages(b, c):
                for n in range(NPG):
                    pg = sp.value_load(pages[0:1, bass.ds(b * NPG + n, 1)], min_val=0, max_val=cache_kv.shape[1] - 1)
                    sp.dma_start(kv[:, c, n, 0:256],
                                 cache_kv[0, bass.ds(pg, 1), :, 2].rearrange("o t g d -> (o t) (g d)")).then_inc(kv_in[c], 16)

            sp.wait_ge(kt_ps, 6)
            for n in range(NPG):
                pg = sp.value_load(pages[0:1, n:n + 1], min_val=0, max_val=cache_kv.shape[1] - 1)
                sp.dma_start(early(n), cache_kv[0, bass.ds(pg, 1), :, 2].rearrange("o t g d -> (o t) (g d)")).then_inc(kv_in[0], 16)

            def load_keys(b, c):
                if type(b) is int and b == 0:
                    return
                if type(b) is not int or b >= 2:
                    sp.wait_ge(e_tp, b * 5 - 5)
                    window_keys(b, c)
                load_pages(b, c)

            def load_values(b, c):
                if type(b) is not int or b >= 2:
                    sp.wait_ge(e_pv, b - 1)
                    window_values(b, c)

            sp.wait_ge(co_ev, 8)
            for b in range(2):
                window_keys(b, b)
                window_values(b, b)
            sp.wait_ge(oz_ready, 4)
            sp.wait_ge(oT_ps, 4)
            staging_order(sp, load_keys, load_values)

            sp.wait_ge(e_pv, NB - 1)
            for m in range(8):
                gp, r = divmod(m, GRP)
                for g2 in range(2):
                    row = (gp * 8 + g2 * 4 + r) * HD
                    sp.dma_start(w_o[g2 * HD:(g2 + 1) * HD, m], nsa_w_out[0, row:row + HD, :]).then_inc(w_o_in, 16)
            sp.wait_ge(e_pv, NB)
            sp.dma_start(gain, ln_g[1:2, :].broadcast_to([P, DM])).then_inc(s_ln, 16)
            sp.dma_start(offs, ln_b[1:2, :].broadcast_to([P, DM])).then_inc(s_ln, 16)
            for t in range(4):
                sp.wait_ge(ln_done, TT + t + 1)
                sp.dma_start(y_prompt[0, t * P:(t + 1) * P], xr[:, t]).then_inc(s_cpy, 16)
            sp.wait_ge(ln_done, 2 * TT)
            sp.dma_start(y_sample.rearrange("b t m -> (b t) m"), xr[0:64, 4, :]).then_inc(s_cpy, 16)
            sp.wait_ge(s_cpy, 112)

        @block.gpsimd
        def _(pool):
            ch = Chain(pool, pool_s)
            ch.mark(pool.memset(ident, 0.0))
            pool.memset(ones, 1.0).then_inc(s_const, 1)
            ch.link(pool.memset(w2pad[:, 0, HD:P], 0.0))
            pool.memset(w2pad[:, 1, 0:HD], 0.0).then_inc(s_const, 1)

            def keep(v, fill, pattern, base, mult, op=ALU.is_ge):
                return pool.affine_select(out=v, in_=v, compare_op=op, fill=fill, base=base, pattern=pattern,
                                          channel_multiplier=mult)
            keep(ident, 1.0, [[-1, P]], 0, 1, ALU.not_equal).then_inc(s_const, 1)
            pool.sem_inc(conv_s, 2)
            pool.wait_ge(rl_ready, 2 * NB)
            pool.wait_ge(xt_used, NB * 16 + 4)
            ch.mark(pool.memset(y_sum, 0.0))
            ch.link(pool.memset(y_sq, 0.0))
            base = ch.base + ch.n
            PER = 1 + TS + 5 + 3
            with pool.Fori(0, CT // 2) as it:
                for c in range(2):
                    ct = it * 2 + c
                    ch.enter(base + ct * PER)
                    pool.wait_ge(conv_s, ct + 2)
                    pool.wait_ge(par_ready, ct + 1)
                    pool.wait_ge(st_up, 2 * ct + 3)
                    for n in range(TS):
                        ch.mark(pool.tensor_tensor(terms[:, :, n, 0:TAPS], ups[c][:, :, n:n + TAPS],
                                                   par[:, c:c + 1, 0:TAPS].broadcast_to([P, NB, TAPS]), ALU.mult))
                    ch.mark(pool.tensor_copy(terms[:, :, :, TAPS], par[:, c, TAPS + 3:TAPS + 4].rearrange(
                        "p (b n) -> p b n", b=1).broadcast_to([P, NB, TS])))
                    pool.wait_ge(pool_s, ch.base + ch.n)
                    flat = terms.rearrange("p b n k -> p (b n) k")
                    for half in (16, 8, 4, 2):
                        ch.link(pool.tensor_tensor(flat[:, :, 0:half], flat[:, :, 0:half], flat[:, :, half:2 * half], ALU.add))
                    ch.link(pool.tensor_tensor(acc[:, TP:TOK], flat[:, :, 0], flat[:, :, 1], ALU.add))
                    pool.tensor_copy(y[:, bass.ds(ct, 1), TP:TOK].rearrange("p c n -> p (c n)"), acc[:, TP:TOK]).then_inc(conv_s, 1)
                    tile = y[:, bass.ds(ct, 1)].rearrange("p c n -> p (c n)")
                    pool.wait_ge(conv_s, ct + 3)
                    pool.wait_ge(conv_done, ct + 3)
                    ch.mark(pool.tensor_tensor(square, tile, tile, ALU.mult))
                    ch.mark(pool.tensor_tensor(y_sum, y_sum, tile, ALU.add))
                    pool.wait_ge(pool_s, ch.base + ch.n)
                    ch.link(pool.tensor_tensor(y_sq, y_sq, square, ALU.add))
                    assert ch.n == PER
            ch.enter(base + CT * PER)

            pool.sem_inc(sums_ready, 1)
            pool.wait_ge(st_sum, 1)
            for v, fill in ((tri, 0.0), (quad, 1.0), (wmask, 0.0), (cmask, 0.0), (cvalid, 1.0)):
                ch.mark(pool.memset(v, fill))
            pool.wait_ge(pool_s, ch.base + ch.n)
            q4 = quad.rearrange("p (a b) -> p a b", b=4)
            ch.mark(keep(q4, 0.0, [[-4, 32], [0, 4]], 0, 1))
            ch.mark(keep(wmask, NEG, [[16, WIN + TS]], -1, -1))
            pool.wait_ge(pool_s, ch.base + ch.n)
            keep(tri, NEG, [[-1, P]], 0, 1).then_inc(masks_ready, 1)
            keep(q4, 0.0, [[4, 32], [0, 4]], 3, -1).then_inc(masks_ready, 1)
            keep(wmask, NEG, [[-16, WIN + TS]], 16 * WIN, 1).then_inc(masks_ready, 1)
            keep(cmask, NEG, [[P, 4], [-STR, PC]], -(2 * STR - 1), 1).then_inc(masks_ready, 1)
            keep(cvalid, 0.0, [[P, 4]], -(2 * STR - 1), 1).then_inc(masks_ready, 1)

            for c in range(CT):
                pool.wait_ge(yn_act, c + 1)
                pool.tensor_tensor(y[:, c], y[:, c], sz[:, c], ALU.mult).then_inc(yn_ready, 1)

            pool.wait_ge(hp_ev, 2)
            pool.memset(vbd, 0.0).then_inc(vbd_zero, 1)
            pool.wait_ge(q_ev_a, 4 + 8)
            pool.wait_ge(q_ev_v, 4 + 8)
            ch.link(pool.memset(qbd, 0.0))
            for m in range(8):
                gp, r = divmod(m, GRP)
                for g2 in range(2):
                    h = slice(g2 * HD, (g2 + 1) * HD)
                    dst = qbd[h].rearrange("p b a (q g r) -> p b a q g r", q=TS, g=NKV)[:, :, gp, :, gp * 2 + g2, r]
                    pool.tensor_copy(dst, qT[h, m, TP:TOK].rearrange("p (b q) -> p b q", b=NB)).then_inc(qbd_ready, 1)
            pool.wait_ge(qbd_ready, 16)
            pool.wait_ge(g_ev, TT)
            for c in range(2):
                for g2 in range(2):
                    ch.mark(pool.memset(qs[c][(1 - g2) * HD:(2 - g2) * HD, g2], 0.0))
            pool.wait_ge(pool_s, ch.base + ch.n)
            for gp in range(2):
                with pool.Fori(0, 2) as it:
                    for c in range(2):
                        blk = it * 2 + (gp * 4 + c)
                        pool.wait_ge(u_sc, blk * 16 + 16)
                        for g2 in range(2):
                            h = slice(g2 * HD, (g2 + 1) * HD)
                            pool.tensor_copy(qs[c][h, g2], qT[h, bass.ds(blk, 1), 0:TP].rearrange("p m t -> p (m t)")
                                             ).then_inc(qs_ready, 1)

            pool.wait_ge(oT_ps, 4)
            pool.wait_ge(qs_ready, 16)

            def stage_queries(b, c):
                if type(b) is not int or b >= 2:
                    pool.wait_ge(e_s, b * 5 - 5)
                pool.tensor_copy(qb[:, c].rearrange("p g n -> p (g n)"), qbd[:, bass.ds(b, 1)].rearrange("p b g n -> p (b g n)")
                                 ).then_inc(q_stage, 1)

            def stage_values(b, c):
                if type(b) is not int or b >= 2:
                    pool.wait_ge(e_pv, b - 1)
                pool.tensor_copy(vcb[0:NC, c], vc[0:NC, bass.ds(b, 1)].rearrange("p b n -> p (b n)")).then_inc(c_stage, 1)
                if type(b) is int and b == 0:
                    pool.wait_ge(e_tp, 5)
                for n in range(NPG):
                    pg = pool.value_load(pages[0:1, bass.ds(b * NPG + n, 1)], min_val=0, max_val=cache_kv.shape[1] - 1)
                    pool.dma_start(kv[:, c, n, 256:512],
                                   cache_kv[0, bass.ds(pg, 1), :, 3].rearrange("o t g d -> (o t) (g d)")).then_inc(vp_in[c], 16)

            staging_order(pool, stage_queries, stage_values)

        @block.scalar
        def _(act):
            for t in range(TT):
                transposed_copy(act, t, 1, s_xps, s_xev, xT)
            act.wait_ge(s_aps, 1)
            act.copy(pars[:, 0:8].rearrange("p c n -> p (c n)"), bank[4][:, 0:8 * NPAR]).then_inc(s_aev, 1)
            act.sem_inc(h_silu, 2)
            act.sem_inc(vc_ev, 1)
            act.sem_inc(gl_free, 1)
            act.sem_inc(st_up, 1)
            act.sem_inc(uo_ready, 1)
            act.sem_inc(state_out[0], 32)
            act.sem_inc(state_out[1], 32)
            act.wait_ge(s_cb, 1)
            with act.Fori(0, NB // 2) as it:
                for c in range(2):
                    b = it * 2 + c

                    def silu(s):
                        act.wait_ge(xt_used, b * 16 + 8 * s + 12)
                        act.wait_ge((kc_ps, vc_ps)[s], b + 1)
                        act.activation(hT[:, s, 0:4 * NC].rearrange("p (g n) -> p g n", g=4),
                                       bank[4 + s][:, :].rearrange("p (g n) -> p g n", g=4)[:, :, 0:NC],
                                       ACT.Silu, bias=cb[:, s:s + 1]).then_inc(h_silu, 1)

                    for n in range(SP2):
                        k = 2 * n + 1
                        act.wait_ge(xp_ready, b * 16 + k + 1)
                        act.wait_ge(xt_used, b * 16 + k + 1)
                        act.copy(xtr[:, k % 4], bank[k % 4][:, :]).then_inc(xt_a, 1)
                        if n == 4:
                            silu(0)
                    silu(1)
                    act.wait_ge(vc_ps, b + 2)
                    act.copy(vc[0:NC, bass.ds(b, 1), :].rearrange("p b v -> p (b v)"), bank[7][0:NC, 0:256]).then_inc(vc_ev, 1)

            with act.Fori(0, CT // 2) as it:
                for c in range(2):
                    ct = it * 2 + c
                    act.wait_ge(conv_done, ct + 1)
                    act.wait_ge(conv_s, ct + 1)
                    act.copy(par[:, c], pars[:, bass.ds(ct, 1), :].rearrange("p c n -> p (c n)")).then_inc(par_ready, 1)
                    act.wait_ge(par_ready, ct + 1)
                    act.wait_ge(gl_ps, ct + 1)
                    act.wait_ge(a_free, ct + 1)
                    for h in range(2):
                        last = act.activation(sgl[:, h * HALF:(h + 1) * HALF], bank[GL + h][:, 0:HALF], ACT.Sigmoid,
                                              bias=par[:, c, TAPS + 1:TAPS + 2])
                    last.then_inc(gl_free, 1)
                    act.wait_ge(st_ps, ct + 1)
                    act.copy(ups[c][:, :, 0:TAPS - 1], bank[4][:, 0:NB * (TAPS - 1)].rearrange("p (b n) -> p b n", b=NB)
                             ).then_inc(st_up, 1)
                    act.wait_ge(a_free, ct + 2)
                    act.copy(ups[c][:, :, TAPS - 1:], usc[:, c].rearrange("p (b n) -> p b n", b=NB)).then_inc(st_up, 1)
                    act.wait_ge(z_ps, ct + 1)
                    act.wait_ge(z_free, ct + 1)
                    for h in range(2):
                        last = act.activation(sgz[:, h * HALF:(h + 1) * HALF], bank[Z + h][:, 0:HALF], ACT.Sigmoid,
                                              bias=par[:, c, TAPS + 2:TAPS + 3])
                    last.then_inc(sgz_ready, 1)
                    act.wait_ge(u_ps, ct + 1)
                    act.wait_ge(state_out[c], it * 32 + 32)
                    act.copy(uo[0:30, c, 0:P], bank[5][0:30, 0:P])
                    act.copy(uo[0:64, c, P:256], bank[5][0:64, P:256]).then_inc(uo_ready, 1)
                    col = it * 256 + c * P
                    act.wait_ge(uo_ready, ct + 2)
                    act.dma_start(state_p[0, 0, :, bass.ds(col, P)], uo[0:30, c, 0:P]).then_inc(state_out[c], 16)
                    act.dma_start(state_s[0, :, TAPS - 1 - TS:TAPS - 1, bass.ds(col, P)], uo[0:64, c, P:256]
                                  ).then_inc(state_out[c], 16)

            for c in range(2):
                act.wait_ge(state_out[c], 16 * CT + 32)
            act.wait_ge(var_ready, 1)
            act.activation(acc, acc, ACT.Sqrt).then_inc(std_ready, 1)
            for c in range(CT):
                act.wait_ge(norm_done, c + 1)
                act.activation(y[:, c], y[:, c], ACT.Silu, bias=pars[:, c, TAPS + 5:TAPS + 6],
                               scale=pars[:, c, TAPS + 4:TAPS + 5]).then_inc(yn_act, 1)
            for t in range(TT):
                deviation(act, t, 2)
                if t:
                    transposed_copy(act, t - 1, 1, x1_ps, x1_ev, xT, X1_PAIRS)
            transposed_copy(act, TT - 1, 1, x1_ps, x1_ev, xT, X1_PAIRS)

            act.sem_inc(q_ev_a, 4)
            act.wait_ge(kv_ev, 3 * TT + 5)
            act.dma_start(kv_p[0, 0].rearrange("(t p) s g d -> p t (s g d)", p=P), kvr[:, 0:4, 0:1024]).then_inc(kv_out, 16)
            act.dma_start(kv_s[0].rearrange("b t s g d -> (b t) (s g d)"), kvr[0:64, 4, 0:1024]).then_inc(kv_out, 16)
            act.dma_start(win_p[0, 0].rearrange("(t p) s g d -> p t (s g d)", p=P), kvr[:, 0:4, 1024:1536]).then_inc(kv_out, 16)
            act.dma_start(win_s[0, :, WIN - TS:WIN].rearrange("b t s g d -> b t (s g d)"), kvr[0:64, 4, 1024:1536]
                          ).then_inc(kv_out, 16)
            with act.Fori(0, 2) as it:
                for r in range(GRP):
                    act.wait_ge(q_ps, it * 7 + (2 * r + 1))
                    act.mul(qT[:, bass.ds(it * 4 + r, 1), 0:HALF].rearrange("p m t -> p (m t)"), bank[2 * r][:, 0:HALF],
                            HD ** -0.5).then_inc(q_ev_a, 1)
            with act.Fori(0, 2) as it:
                for t in range(TT):
                    n = ROWS[t]
                    if t < TT - 1:
                        act.wait_ge(zz_ps, it * 4 + (t + 1))
                    else:
                        act.wait_ge(ring_used, it * RING + (CT + 6 * RING))
                    act.wait_ge(zz_ev, it * 5 + (t + 4 + (t == 0)))
                    act.activation(sig[0:n, t % 2], bank[t][0:n, :], ACT.Sigmoid).then_inc(zz_sg, 1)
            for t in range(TT):
                n = ROWS[t]
                if t < TT - 1:
                    act.wait_ge(g_ps, t + 1)
                else:
                    act.wait_ge(ring_used, CT + 8 * RING)
                act.activation(gates[0:n, t].rearrange("p h j -> p (h j)"), bank[t][0:n, 0:48], ACT.Sigmoid).then_inc(g_ev, 1)
            for n in (1, 3):
                act.wait_ge(kt_ps, n + 1)
                act.copy(ktp[:, n // 2, n % 2], bank[4 + n][:, :]).then_inc(kt_ev_a, 1)
            act.wait_ge(kt_ps, 6)
            act.copy(zts.rearrange("p m n -> p (m n)"), bank[1][:, :]).then_inc(kt_ev_a, 1)
            for n in (1, 3):
                act.wait_ge(xtp_ps, n + 1)
                act.copy(xtp[:, 4 * n:4 * n + 4].rearrange("p k g n -> p (k g n)"), bank[4 + n][:, :]).then_inc(xtp_ev_a, 1)
            for st_ in range(2):
                act.wait_ge(hp_ps, st_ + 1)
                act.activation(htp[:, st_, 0:4 * PCN], bank[2 + st_][:, 0:4 * PCN], ACT.Silu, bias=cb[:, st_:st_ + 1]
                               ).then_inc(hp_ev, 1)
            for i in range(5):
                if i < 4:
                    act.wait_ge(cs_mx, i + 1)
                    act.activation(pc[i % 2], pc[i % 2], ACT.Exp).then_inc(cs_ex, 1)
                if i:
                    act.wait_ge(ct_ps, i)
                    if i > 1:
                        act.wait_ge(co_ps, i - 1)
                    act.copy(pcT, bank[4 + (i - 1) % 2][:, :]).then_inc(ct_ev, 1)
            for gp in range(2):
                with act.Fori(0, 2) as it:
                    g0 = it * 32 + gp * 64
                    for u in range(33):
                        if u < 32:
                            n = (UNITS[u][1] + 1) * P
                            act.wait_ge(u_mx, g0 + (u + 1))
                            if u >= 3:
                                act.wait_ge(u_tp, g0 + (u - 2))
                            act.activation(prob[:, u % 3, 0:n], bank[u % 3][:, 0:n], ACT.Exp, bias=ust[:, u % 4:u % 4 + 1],
                                           accum_out=ust[:, 4 + u % 4:5 + u % 4]).then_inc(u_ex, 1)
                        if u >= 1:
                            v = u - 1
                            n = (UNITS[v][1] + 1) * P
                            act.wait_ge(u_tp, g0 + u)
                            if v >= 2:
                                act.wait_ge(u_pv, g0 + (v - 1))
                            act.copy(probT[:, v % 2, 0:n], bank[3 + v % 2][:, 0:n]).then_inc(u_pt, 1)
            for t in range(4):
                transposed_copy(act, t, 1, oT_ps, oT_ev, oT)

            def turned(b, n):
                act.wait_ge(e_tp, b * 5 + (n + 1))
                if n >= 2:
                    act.wait_ge(e_s, b * 5 + (n - 1))
                for g in range(2):
                    act.copy(ktb[n % 2][:, g], bank[3 + g][:, :]).then_inc(e_te, 1)

            def exponentials(b, c, n):
                act.wait_ge(e_nm, b * 2 + (n + 1))
                v = pb[c][:, 2056:2576] if n == 0 else pb[c][:, 0:2056]
                act.activation(v, v, ACT.Exp, bias=sst[:, 8 + n:9 + n], accum_out=sst[:, 10 + n:11 + n]).then_inc(e_ex, 1)

            def weights_out(b, n):
                act.wait_ge(e_pp, b * 7 + (n + 1))
                if n == 1:
                    act.copy(pt[0:TS, n % 4, 0:P], bank[7][0:TS, 0:P])
                    act.copy(pt[0:NC, n % 4, P:2 * P], bank[7][0:NC, P:2 * P]).then_inc(e_pt_a, 1)
                else:
                    act.copy(pt[:, n % 4], bank[7][:, :]).then_inc(e_pt_a, 1)

            def step(b, c, scores=True, output=True):
                if scores:
                    turned(b, 0)
                if output:
                    exponentials(b - 1, 1 - c, 1)
                if scores:
                    turned(b, 1)
                    act.wait_ge(e_cm, b + 2)
                    act.activation(pcn, bank[0][:, 0:NC], ACT.Exp, bias=sst[:, 0:1], accum_out=sst[:, 1:2]).then_inc(e_cx, 1)
                for n in (2, 3, 4):
                    if scores:
                        turned(b, n)
                    if output:
                        weights_out(b - 1, 2 * n - 3)
                if scores:
                    exponentials(b, c, 0)

            sample_order(act, step)
            for t in range(TT):
                deviation(act, t, 2 + TT)


        @block.vector
        def _(dve):
            ch = Chain(dve, dve_s)
            for t in range(TT):
                transposed_copy(dve, t, 0, s_xps, s_xev, xT)
            dve.wait_ge(s_aps, 1)
            ch.mark(dve.tensor_copy(pars[:, 8:16].rearrange("p c n -> p (c n)"), bank[5][:, 0:8 * NPAR]))
            dve.tensor_copy(auxT, bank[6][:, 0:34]).then_inc(s_aev, 1)
            dve.wait_ge(s_cbp, 1)
            dve.wait_ge(s_aev, 2)
            dve.tensor_tensor(cb, bank[7][:, 0:2], auxT[:, 32:34], ALU.add).then_inc(s_cb, 1)
            dve.sem_inc(xt_used, 4)
            dve.sem_inc(kc_ev, 1)
            dve.sem_inc(a_free, 1)
            dve.sem_inc(z_free, 1)
            dve.sem_inc(conv_done, 2)

            def regroup(b, c, s):
                dve.tensor_copy(rl[:, s].rearrange("p g q n -> p g (q n)").rearrange("p g (t d) -> p g t d", d=HD),
                                xc[:, c].rearrange("p t (s g d) -> p s g t d", s=2, g=NKV)[:, s]).then_inc(rl_ready, 1)

            dve.wait_ge(s_aps, 1)
            dve.wait_ge(xc_in[0], 256)
            for s in range(2):
                regroup(0, 0, s)

            def compress_copies(it, last):
                for c in range(2):
                    b = it * 2 + c
                    for n in range(SP2):
                        k = 2 * n
                        dve.wait_ge(xp_ready, b * 16 + k + 1)
                        dve.wait_ge(xt_used, b * 16 + k + 1)
                        dve.tensor_copy(xtr[:, k % 4], bank[k % 4][:, :]).then_inc(xt_v, 1)
                        if n in (4, 7) and not (last and c):
                            if n == 4:
                                dve.wait_ge(xc_in[1 - c], (it + c) * 256 + 256)
                            s = n // 7
                            dve.wait_ge(xp_ready, b * 16 + 8 * s + 8)
                            regroup(b + 1, 1 - c, s)
                    dve.wait_ge(kc_ps, b + 2)
                    dve.tensor_copy(kcT[:, bass.ds(b, 1)].rearrange("p b g n -> p (b g n)"), bank[6][:, 0:2 * NC]
                                    ).then_inc(kc_ev, 1)

            with dve.Fori(0, NB // 2 - 1) as it:
                compress_copies(it, False)
            compress_copies(NB // 2 - 1, True)

            for c in range(2):
                ch.mark(dve.memset(upp[c][:, 0:CONV_AHEAD], 0.0))
            setup = ch.n
            dve.wait_ge(dve_s, setup)
            PER = TAPS
            with dve.Fori(0, CT // 2) as it:
                for c in range(2):
                    ct = it * 2 + c
                    ch.enter(setup + ct * PER)
                    ba, bz, bw = (par[:, c, n:n + 1] for n in (TAPS, TAPS + 2, TAPS + 3))
                    dve.wait_ge(par_ready, ct + 1)
                    dve.wait_ge(a_ps, ct + 1)
                    dve.wait_ge(gl_free, ct + 2)
                    rest = TP - HALF
                    dve.scalar_tensor_tensor(upp[c][:, CONV_AHEAD:CONV_AHEAD + HALF], bank[A][:, 0:HALF], ba,
                                             sgl[:, 0:HALF], ALU.add, ALU.mult)
                    dve.scalar_tensor_tensor(upp[c][:, CONV_AHEAD + HALF:], bank[A + 1][:, 0:rest], ba,
                                             sgl[:, HALF:TP], ALU.add, ALU.mult)
                    dve.scalar_tensor_tensor(
                        usc[:, c], bank[A + 1][:, rest:HALF], ba, sgl[:, TP:TOK], ALU.add, ALU.mult).then_inc(a_free, 1)
                    dve.wait_ge(a_free, ct + 2)
                    yp, _ = split(acc)
                    op, _ = split(y[:, bass.ds(ct, 1)].rearrange("p c t -> p (c t)"))
                    for k in range(TAPS):
                        w = par[:, c, k:k + 1]
                        src = upp[c][:, k:k + TP]
                        part = (yp, acc_odd)[k % 2]
                        if k == 0:
                            ch.mark(dve.tensor_scalar(part, src, w, bw, ALU.mult, ALU.add))
                        elif k == 1:
                            ch.mark(dve.tensor_scalar(part, src, w, None, ALU.mult))
                        else:
                            dve.wait_ge(dve_s, ch.base + (ch.n - 1))
                            ch.mark(dve.scalar_tensor_tensor(part, src, w, part, ALU.mult, ALU.add))
                        if k == 16:
                            dve.wait_ge(sgz_ready, ct + 1)
                            for h in range(2):
                                n0 = h * HALF
                                ins = dve.scalar_tensor_tensor(
                                    sz[:, bass.ds(ct, 1), n0:n0 + HALF].rearrange("p c t -> p (c t)"), bank[Z + h][:, 0:HALF], bz,
                                    sgz[:, n0:n0 + HALF], ALU.add, ALU.mult)
                            ins.then_inc(z_free, 1)
                    dve.wait_ge(dve_s, ch.base + ch.n)
                    dve.tensor_tensor(op, yp, acc_odd, ALU.add).then_inc(conv_done, 1)
                    assert ch.n == PER
            ch.enter(setup + CT * PER)

            mu, rstd, tmp = sgl, acc, sgz
            dve.wait_ge(st_sum, 1)
            dve.wait_ge(conv_s, CT + 2)
            dve.wait_ge(conv_done, CT + 2)
            for h in range(2):
                ch.mark(dve.tensor_scalar(mu[:, h * HALF:(h + 1) * HALF], bank[h][:, 0:HALF], 1.0 / DIN, None, ALU.mult))
            dve.wait_ge(dve_s, ch.base + ch.n)
            ch.link(dve.tensor_tensor(tmp, mu, mu, ALU.mult))
            for h in range(2):
                ch.mark(dve.scalar_tensor_tensor(rstd[:, h * HALF:(h + 1) * HALF], bank[2 + h][:, 0:HALF], 1.0 / DIN,
                                                 tmp[:, h * HALF:(h + 1) * HALF], ALU.mult, ALU.subtract))
            dve.wait_ge(dve_s, ch.base + ch.n)
            dve.tensor_scalar(rstd, rstd, EPS, None, ALU.add).then_inc(var_ready, 1)
            dve.wait_ge(std_ready, 1)
            ch.link(dve.reciprocal(rstd, rstd))
            for c in range(CT):
                ch.link(dve.tensor_tensor(y[:, c], y[:, c], mu, ALU.subtract))
                dve.tensor_tensor(y[:, c], y[:, c], rstd, ALU.mult).then_inc(norm_done, 1)

            for t in range(TT):
                if t < TT - 1:
                    dve.wait_ge(o_ps, t + 1)
                else:
                    dve.wait_ge(ring_used, CT)
                residual(dve, ch, t, 0, bank[t], t + 1)
            for t in range(TT):
                dve.wait_ge(o_ps, TT + t)
                residual(dve, ch, t, 1, bank[t], TT + t + 1)
                normalise(dve, ch, t, 32, 2)
                if t:
                    transposed_copy(dve, t - 1, 0, x1_ps, x1_ev, xT, X1_PAIRS)
            transposed_copy(dve, TT - 1, 0, x1_ps, x1_ev, xT, X1_PAIRS)

            dve.sem_inc(kv_ev, 5)
            dve.sem_inc(q_ev_v, 4)
            dve.sem_inc(zz_ev, 5)
            with dve.Fori(0, 3) as it:
                for t in range(TT):
                    n = ROWS[t]
                    if t < TT - 1:
                        dve.wait_ge(kv_ps, it * 4 + (t + 1))
                    else:
                        dve.wait_ge(ring_used, it * RING + (CT + RING))
                    dve.tensor_copy(kvr[0:n, t, bass.ds(it * 512, 512)], bank[t][0:n, :]).then_inc(kv_ev, 1)
            with dve.Fori(0, 2) as it:
                for r in range(GRP):
                    if r < GRP - 1:
                        dve.wait_ge(q_ps, it * 7 + (2 * r + 2))
                    else:
                        dve.wait_ge(ring_used, it * RING + (CT + 4 * RING))
                    dve.tensor_scalar(qT[:, bass.ds(it * 4 + r, 1), HALF:TOK].rearrange("p m t -> p (m t)"),
                                      bank[2 * r + 1][:, 0:HALF], HD ** -0.5, None, ALU.mult).then_inc(q_ev_v, 1)
            with dve.Fori(0, 2) as it:
                for t in range(TT):
                    n = ROWS[t]
                    dve.wait_ge(zz_sg, it * 5 + (t + 1))
                    dve.tensor_tensor(zr[0:n, t, bass.ds(it * 512, 512)], bank[t][0:n, :], sig[0:n, t % 2], ALU.mult
                                      ).then_inc(zz_ev, 1)
            for n in (0, 2):
                dve.wait_ge(kt_ps, n + 1)
                dve.tensor_copy(ktp[:, n // 2, n % 2], bank[4 + n][:, :]).then_inc(kt_ev, 1)
            dve.wait_ge(kt_ps, 5)
            dve.tensor_copy(kts.rearrange("p s g n -> p (s g n)"), bank[0][:, 0:256]).then_inc(kt_ev, 1)
            for n in (0, 2):
                dve.wait_ge(xtp_ps, n + 1)
                dve.tensor_copy(xtp[:, 4 * n:4 * n + 4].rearrange("p k g n -> p (k g n)"), bank[4 + n][:, :]).then_inc(xtp_ev_v, 1)
            dve.wait_ge(xtp_ps, 4)
            ch.link(dve.memset(kctp, 0.0))
            dve.wait_ge(w2p_ps, 1)
            for g2 in range(2):
                h = slice(g2 * HD, (g2 + 1) * HD)
                dve.tensor_copy(kctp[h, :, g2, 0:PCN], bank[0][h, 0:2 * PCN].rearrange("p (g n) -> p g n", g=2)).then_inc(w2p_ev, 1)
            dve.wait_ge(w2p_ps, 2)
            dve.tensor_copy(vcp[0:PCN], bank[1][0:PCN, 0:256]).then_inc(w2p_ev, 1)

            dve.wait_ge(masks_ready, 5)
            def each(v):
                return v.rearrange("p (h o) -> p h o", o=1).broadcast_to([P, NH, PC])

            def subtract_maxima(i):
                v, st_ = pc[i % 2], cst[i % 2]
                dve.wait_ge(cs_ps, i + 1)
                if i >= 2:
                    dve.wait_ge(ct_ps, i - 1)
                v5 = v.rearrange("p (a g r n) -> p a g r n", a=2, g=2, r=GRP)
                for g2 in range(2):
                    for gp in range(2):
                        ch.mark(dve.tensor_tensor(v5[:, gp, g2], bank[i][:, :].rearrange(
                            "p (a r g n) -> p a g r n", a=2, r=GRP, g=2)[:, gp, g2], cmask[:, i:i + 1, :].broadcast_to([P, GRP, PC]), ALU.add))
                dve.wait_ge(dve_s, ch.base + ch.n)
                v3 = v.rearrange("p (h n) -> p h n", h=NH)
                ch.link(dve.tensor_reduce(st_[:, 0:16], v3, AX, ALU.max))
                dve.tensor_tensor(v3, v3, each(st_[:, 0:16]), ALU.subtract).then_inc(cs_mx, 1)

            def weigh(i):
                v3, st_ = pc[i % 2].rearrange("p (h n) -> p h n", h=NH), cst[i % 2]
                dve.wait_ge(cs_ex, i + 1)
                ch.link(dve.tensor_reduce(st_[:, 16:32], v3, AX, ALU.add))
                ch.link(dve.reciprocal(st_[:, 32:48], st_[:, 16:32]))
                ch.link(dve.scalar_tensor_tensor(st_[:, 48:64], st_[:, 32:48], cvalid[:, i:i + 1], gates[:, i, :, 0],
                                                 ALU.mult, ALU.mult))
                dve.tensor_tensor(v3, v3, each(st_[:, 48:64]), ALU.mult).then_inc(cs_sc, 1)

            def take_out(i):
                for gp in range(2):
                    dve.wait_ge(co_ps, i + 1)
                    dve.tensor_copy(att[:, i, gp * 4:gp * 4 + 4].rearrange("p r g d -> p g r d"),
                                    bank[6 + gp][:, :].rearrange("p (g r d) -> p g r d", g=2, r=GRP)).then_inc(co_ev, 1)

            subtract_maxima(0)
            for i in range(4):
                if i < 3:
                    subtract_maxima(i + 1)
                weigh(i)
                if i:
                    take_out(i - 1)
            take_out(3)

            dve.sem_inc(u_fo, 3)
            dve.wait_ge(co_ev, 8)
            u0 = ch.n + ch.base
            for gp in range(2):
                with dve.Fori(0, 2) as it:
                    ch.enter(it * 96 + (u0 + gp * 192))
                    g0 = it * 32 + gp * 64
                    for u in range(35):
                        fin = u - 3
                        k = fin % 4
                        if fin >= 0:
                            c, g2, i, br = UNITS[fin][3], UNITS[fin][0], UNITS[fin][1], UNITS[fin][2]
                            dve.wait_ge(u_ex, g0 + (fin + 1))
                            at_rec = ch.mark(dve.reciprocal(ust[:, 8 + k:9 + k], ust[:, 4 + k:5 + k]))
                        if u < 32:
                            n = (UNITS[u][1] + 1) * P
                            dve.wait_ge(u_sc, g0 + (33 + u))
                            at_tri = ch.mark(dve.tensor_tensor(bank[u % 3][:, n - P:n], bank[u % 3][:, n - P:n], tri, ALU.add))
                        if fin >= 0:
                            dve.wait_ge(dve_s, at_rec)
                            gcol = (gp * 8 + g2 * 4 + c) * 3 + 1 + br
                            gate = gates[:, i].rearrange("p h j -> p (h j)")[:, bass.ds(it * 6 + gcol, 1)]
                            at_gate = ch.mark(dve.tensor_tensor(ust[:, 12 + k:13 + k], ust[:, 8 + k:9 + k], gate, ALU.mult))
                        if u < 32:
                            dve.wait_ge(dve_s, at_tri)
                            dve.tensor_reduce(ust[:, u % 4:u % 4 + 1], bank[u % 3][:, 0:n], AX, ALU.max, negate=True
                                              ).then_inc(u_mx, 1)
                        if fin >= 0:
                            dve.wait_ge(dve_s, at_gate)
                            dve.wait_ge(u_pv, g0 + (fin + 1))
                            o = att[:, i, bass.ds(it * 2 + (gp * 4 + c), 1), g2].rearrange("p m d -> p (m d)")
                            if br:
                                dve.wait_ge(u_fo, g0 + (fin + 3))
                            dve.scalar_tensor_tensor(o, bank[5 + fin % 3][:, 0:HD], ust[:, 12 + k:13 + k], o, ALU.mult, ALU.add
                                                     ).then_inc(u_fo, 1)
                    assert ch.n == 96
            ch.enter(u0 + 384)
            dve.wait_ge(u_fo, 128 + 3)
            for i in range(4):
                row = att[:, i].rearrange("p m g d -> p (m g d)")
                dve.tensor_tensor(row, row, zr[:, i], ALU.mult).then_inc(oz_ready, 1)
            for t in range(4):
                transposed_copy(dve, t, 0, oT_ps, oT_ev, oT)

            score, work, top, top2, pick = sel[:, 0:33], sel[:, 33:66], sel[:, 66:74], sel[:, 74:82], sel[:, 82:115]
            dve.sem_inc(e_cm, 1)
            dve.sem_inc(e_ma, 1)
            dve.sem_inc(e_oz, 1)
            dve.wait_ge(oT_ps, 4)
            dve.wait_ge(gr_in, 16)
            ch.mark(dve.memset(score[:, 0:1], BIG))
            ch.link(dve.memset(score[:, 31:33], BIG))

            def gate(b, j):
                return gs[:, bass.ds(b, 1), j]

            def step(b, c, scores=True, output=True):
                p, last = pb[c], pb[1 - c]
                parts = (last[:, 2056:2576], last[:, 0:2056])

                def scale(n):
                    dve.wait_ge(e_ex, b * 2 + (n - 1))
                    ch.link(dve.reciprocal(sst[:, 12 + n:13 + n], sst[:, 10 + n:11 + n]))
                    ch.link(dve.tensor_tensor(sst[:, 14 + n:15 + n], sst[:, 12 + n:13 + n], gate(b - 1, 2 - n), ALU.mult))
                    dve.tensor_scalar(parts[n], parts[n], sst[:, 14 + n:15 + n], None, ALU.mult).then_inc(e_scl, 1)

                def masked(n):
                    dve.wait_ge(e_s, b * 5 + (n + 1))
                    k0 = (n - 1) * 512
                    dve.scalar_tensor_tensor(
                        p[:, k0:k0 + 512].rearrange("p (j o) -> p j o", o=BLK),
                        pick[:, (n - 1) * 8:n * 8].rearrange("p (j o) -> p j o", o=1).broadcast_to([P, 8, BLK]), -NEG,
                        s_bank[n][:, :].rearrange("p (j o) -> p j o", o=BLK), ALU.mult, ALU.add).then_inc(e_ma, 1)

                def weights_out(n):
                    dve.wait_ge(e_pp, b * 7 + (n - 6))
                    if n == 6:
                        dve.tensor_copy(pt[0:TS, n % 4, 0:P], bank[7][0:TS, 0:P]).then_inc(e_pt_v, 1)
                    else:
                        dve.tensor_copy(pt[:, n % 4], bank[7][:, :]).then_inc(e_pt_v, 1)

                if output:
                    dve.wait_ge(e_ma, b * 5 + 1)
                    ch.link(dve.tensor_reduce(sst[:, 23:24], last[:, 1536:2056], AX, ALU.max, negate=True))
                    dve.tensor_reduce(sst[:, 9:10], sst[:, 20:24], AX, ALU.min).then_inc(e_nm, 1)
                if scores:
                    dve.wait_ge(e_sc, b + 1)
                    dve.tensor_tensor(p[:, PAST:PAST + TS], bank[0][:, 128:136], wmask[:, WIN:WIN + TS], ALU.add)
                    dve.tensor_tensor(p[:, 2056 + WIN:2576], bank[0][:, 136:144], wmask[:, WIN:WIN + TS], ALU.add)
                    dve.tensor_reduce(sst[:, 0:1], bank[0][:, 0:NC], AX, ALU.max, negate=True).then_inc(e_cm, 1)
                if output:
                    scale(0)
                if scores:
                    dve.wait_ge(e_cx, b + 1)
                    ch.link(dve.reciprocal(sst[:, 2:3], sst[:, 1:2]))
                    dve.tensor_scalar(pcn, pcn, sst[:, 2:3], None, ALU.mult).then_inc(e_cn, 1)
                if output:
                    scale(1)
                    weights_out(0)
                if scores:
                    dve.wait_ge(e_cn, b + 1)
                    ch.mark(dve.tensor_scalar(p[:, 2576:2576 + NC], pcn, gate(b, 0), None, ALU.mult))
                    dve.wait_ge(e_s, b * 5 + 1)
                    dve.tensor_tensor(p[:, 2056:2056 + WIN], s_bank[0][:, :], wmask[:, 0:WIN], ALU.add).then_inc(e_ma, 1)
                    dve.wait_ge(e_ma, b * 5 + 2)
                    dve.tensor_reduce(sst[:, 8:9], p[:, 2056:2576], AX, ALU.max, negate=True).then_inc(e_nm, 1)
                    dve.wait_ge(e_q4, b + 1)
                    ch.mark(dve.tensor_reduce(work[:, 0:30], bank[0][:, 260:380].rearrange("p (j o) -> p j o", o=4)[:, :, 0:3], AX, ALU.add))
                    ch.mark(dve.tensor_copy(pick[:, 0:30], bank[0][:, 259:379:4]))
                    ch.link(dve.tensor_copy(q7, bank[0][:, 263:383:4]))
                    ch.link(dve.tensor_tensor(pick[:, 0:30], pick[:, 0:30], q7, ALU.add))
                    ch.link(dve.scalar_tensor_tensor(score[:, 1:31], pick[:, 0:30], 0.5, work[:, 0:30], ALU.mult, ALU.add))
                    for k, ranked in enumerate((lambda: dve.max(top, score), lambda: dve.match_replace(work, top, score, -1.0),
                                                lambda: dve.max(top2, work), lambda: dve.match_replace(pick, top2, work, -1.0))):
                        ch.mark(dve.memset(sst[:, 16 + k:17 + k], 0.0))
                        ch.link(ranked())
                    ch.link(dve.tensor_scalar(pick, pick, -1.0, 1.0, ALU.is_equal, ALU.subtract))
                for n in (1, 2, 3):
                    if scores:
                        masked(n)
                    if output and n > 1:
                        weights_out(2 * n - 2)
                    if scores:
                        dve.wait_ge(e_ma, b * 5 + (n + 2))
                        ch.mark(dve.tensor_reduce(sst[:, 19 + n:20 + n], p[:, (n - 1) * 512:n * 512], AX, ALU.max, negate=True))
                if output:
                    weights_out(6)
                    dve.wait_ge(e_pv, b)
                    for gp in range(2):
                        for g2 in range(2):
                            h = slice(g2 * HD, (g2 + 1) * HD)
                            dve.tensor_tensor(
                                oT[h, gp * 4:gp * 4 + 4, bass.ds(b * TS + (TP - TS), TS)].rearrange("p r q -> p q r"),
                                bank[5 + gp][h, 0:64].rearrange("p (q g r) -> p q g r", q=TS, g=2)[:, :, g2],
                                zts[h, gp * 4:gp * 4 + 4, bass.ds(b * TS - TS, TS)].rearrange("p r q -> p q r"), ALU.mult
                                ).then_inc(e_oz, 1)
                if scores:
                    masked(4)

            sample_order(dve, step, ch)

            for t in range(TT):
                for nh in range(2):
                    dve.wait_ge(o2_ps, 2 * t + nh + 1)
                    residual(dve, ch, t, nh, bank[(2 * t + nh) % 8], 2 * TT + 2 * t + nh + 1)
                normalise(dve, ch, t, 64, 2 + TT)

        @block.tensor
        def _(pe):
            pe.wait_ge(s_const, 3)
            pe.wait_ge(s_x, 32)
            for t in range(TT):
                transpose_tile(pe, x_columns, t, PAIRS, s_xps, s_xev)
            pe.wait_ge(s_small, 160)
            for c in range(CT):
                pe.transpose(bank[4 + c // 8][:, (c % 8) * NPAR:(c % 8 + 1) * NPAR], aux[0:NPAR, c * P:(c + 1) * P],
                             ident[0:NPAR, 0:NPAR])
            pe.transpose(bank[6][:, 0:34], aux2[0:34, :], ident[0:34, 0:34]).then_inc(s_aps, 1)
            pe.wait_ge(s_wc, 32)
            pe.wait_ge(s_aev, 2)
            for s in range(2):
                for n in range(16):
                    last = pe.matmul(bank[7][:, s:s + 1], wc[:, s, n // 8, n % 8], auxT[:, s * 16 + n:s * 16 + n + 1],
                                     start=n == 0, stop=n == 15)
            last.then_inc(s_cbp, 1)
            pe.wait_ge(s_cb, 1)
            for w in range(2):
                pe.wait_ge(s_xev[w], TT)
            pe.sem_inc(kc_ps, 1)
            pe.sem_inc(vc_ps, 1)

            with pe.Fori(0, NB // 2) as it:
                for c in range(2):
                    b = it * 2 + c

                    def turn(k):
                        s, q = divmod(k, SP2)
                        if q == 0:
                            pe.wait_ge(rl_ready, b * 2 + s + 1)
                        for g in range(NKV):
                            last = pe.transpose(bank[k % 4][:, g * P:(g + 1) * P], rl[:, s, g, q], ident)
                        last.then_inc(xp_ready, 1)

                    turn(0)
                    for k in range(16):
                        s, q = divmod(k, SP2)
                        if k < 15:
                            turn(k + 1)
                        if q == 0:
                            pe.wait_ge(h_silu, b * 2 + s + 1)
                        pe.wait_ge((xt_v, xt_a)[k % 2], b * 8 + k // 2 + 1)
                        h = bank[4 + s][:, :].rearrange("p (g n) -> p g n", g=4)[:, :, 0:NC]
                        x4 = xtr[:, k % 4].rearrange("p (g n) -> p g n", g=4)
                        for j in range(2):
                            last = pe.matmul(h, wc[:, s, j, q], x4[:, :, j:j + NC], start=(q == 0 and j == 0),
                                             stop=(q == SP2 - 1 and j == 1))
                        last.then_inc(xt_used, 1)
                    pe.wait_ge(h_silu, b * 2 + 3)
                    pe.wait_ge(kc_ev, b + 1)
                    hk = hT[:, 0, 0:4 * NC].rearrange("p (a g n) -> p a g n", a=2, g=2)
                    for g in range(2):
                        last = pe.matmul(bank[6][:, 0:2 * NC].rearrange("p (a n) -> p a n", a=2), w2pad[:, g], hk[:, :, g],
                                         start=g == 0, stop=g == 1)
                    last.then_inc(kc_ps, 1)
                    pe.wait_ge(h_silu, b * 2 + 4)
                    pe.wait_ge(vc_ev, b + 1)
                    for g in range(NKV):
                        last = pe.matmul(bank[7][0:NC, g * HD:(g + 1) * HD], hT[:, 1, g * NC:(g + 1) * NC], w2v,
                                         start=True, stop=True)
                    last.then_inc(vc_ps, 1)

            pe.wait_ge(vc_ev, NB + 1)
            pe.wait_ge(kc_ev, NB + 1)
            pe.wait_ge(xt_v, NB * 8)
            pe.wait_ge(xt_a, NB * 8)
            with pe.Fori(0, CT // 2) as it:
                for c in range(2):
                    ct = it * 2 + c

                    def product(pair, part, ready):
                        for h in range(2):
                            for k in range(KT):
                                last = pe.matmul(bank[pair + h][:, 0:HALF], wi[:, c, part, k], xT[:, k, h * HALF:(h + 1) * HALF],
                                                 start=k == 0, stop=k == KT - 1)
                        last.then_inc(ready, 1)

                    pe.wait_ge(wi_in[c], it * 64 + 64)
                    pe.wait_ge(gl_free, ct + 1)
                    product(GL, 1, gl_ps)
                    pe.wait_ge(st_up, 2 * ct + 1)
                    for h in range(2):
                        last = pe.transpose(bank[4][:, h * 120:(h + 1) * 120], st[0:120, c, h], ident[0:120, 0:120])
                    last.then_inc(st_ps, 1)
                    pe.wait_ge(a_free, ct + 1)
                    product(A, 0, a_ps)
                    pe.wait_ge(z_free, ct + 1)
                    product(Z, 2, z_ps)
                    pe.wait_ge(a_free, ct + 2)
                    pe.wait_ge(uo_ready, ct + 1)
                    pe.transpose(bank[5][0:30, 0:P], upp[c][:, TP:TP + CONV_AHEAD], ident)
                    pe.transpose(bank[5][0:64, P:256], usc[:, c], ident).then_inc(u_ps, 1)

            pe.wait_ge(z_free, CT + 1)
            pe.wait_ge(sums_ready, 1)
            for h in range(2):
                pe.matmul(bank[h][:, 0:HALF], ones, y_sum[:, h * HALF:(h + 1) * HALF], start=True, stop=True)
                last = pe.matmul(bank[2 + h][:, 0:HALF], ones, y_sq[:, h * HALF:(h + 1) * HALF], start=True, stop=True)
            last.then_inc(st_sum, 1)

            for c in range(CT):
                pe.wait_ge(yn_ready, c + 1)
                pe.wait_ge(ring_in[c % RING], 16 * (c // RING + 1))
                for t in range(TT):
                    r = ROWS[t]
                    last = pe.matmul(bank[t][0:r, :], y[:, c, t * P:t * P + r], ring[:, c % RING], start=c == 0,
                                     stop=c == CT - 1)
                    if t == TT - 1:
                        last.then_inc(ring_used, 1)
                    elif c == CT - 1:
                        last.then_inc(o_ps, 1)
            pe.wait_ge(wx_in, 16)
            for t in range(TT):
                r = ROWS[t]
                pe.wait_ge(o_free, t + 1)
                for c in range(CT):
                    last = pe.matmul(bank[t][0:r, :], y[:, c, t * P:t * P + r], wx[:, c], start=c == 0, stop=c == CT - 1)
                last.then_inc(o_ps, 1)
                if t:
                    transpose_tile(pe, x_columns, t - 1, X1_PAIRS, x1_ps, x1_ev, ln_done)

            transpose_tile(pe, x_columns, TT - 1, X1_PAIRS, x1_ps, x1_ev, ln_done)
            for w in range(2):
                pe.wait_ge(x1_ev[w], TT)

            def x_tile(k, t):
                return xT[:, k, t * P:t * P + ROWS[t]]

            with pe.Fori(0, 3) as it:
                for k in range(KT):
                    pe.wait_ge(ring_in[k], it * 16 + 48)
                    token_product(pe, x_tile, k, ring[:, k], 512, k == 0, k == KT - 1,
                                  lambda t: pe.wait_ge(kv_ev, it * 5 + (t + 1)), kv_ps).then_inc(ring_used, 1)
            pe.wait_ge(kv_ev, 20)
            with pe.Fori(0, 2) as it:
                for k in range(KT):
                    pe.wait_ge(ring_in[k], it * 32 + 112)
                    for r in range(GRP):
                        if k == 0:
                            pe.wait_ge(q_ev_a, it * 4 + (r + 1))
                            pe.wait_ge(q_ev_v, it * 4 + (r + 1))
                        for h in range(2):
                            last = pe.matmul(bank[2 * r + h][:, 0:HALF], ring[:, k, r * P:(r + 1) * P],
                                             xT[:, k, h * HALF:(h + 1) * HALF], start=k == 0, stop=k == KT - 1)
                            if r == GRP - 1 and h == 1:
                                last.then_inc(ring_used, 1)
                            elif k == KT - 1:
                                last.then_inc(q_ps, 1)
            pe.wait_ge(q_ev_a, 12)
            pe.wait_ge(q_ev_v, 12)
            with pe.Fori(0, 2) as it:
                for k in range(KT):
                    pe.wait_ge(ring_in[k], it * 32 + 176)
                    token_product(pe, x_tile, k, ring[:, k], 512, k == 0, k == KT - 1,
                                  lambda t: pe.wait_ge(zz_ev, it * 5 + (t + 1)), zz_ps).then_inc(ring_used, 1)
            for k in range(KT):
                pe.wait_ge(ring_in[k], 224)
                token_product(pe, x_tile, k, ring[:, k, 0:48], 48, k == 0, k == KT - 1,
                              lambda t: pe.wait_ge(zz_ev, 11 + t), g_ps).then_inc(ring_used, 1)
            pe.wait_ge(g_ev, TT)
            pe.sem_inc(u_sc, 32)
            for n in range(4):
                for t in range(4):
                    col = (2 + 2 * (n // 2)) * 256 + (n % 2) * P
                    last = pe.transpose(bank[4 + n][:, t * P:(t + 1) * P], kvr[:, t, col:col + P], ident)
                last.then_inc(kt_ps, 1)
            for n in range(4):
                col = (2 + 2 * (n // 2)) * 256 + (n % 2) * P
                last = pe.transpose(bank[0][:, n * 64:(n + 1) * 64], kvr[0:64, 4, col:col + P], ident[0:64, 0:64])
            last.then_inc(kt_ps, 1)
            for m in range(8):
                last = pe.transpose(bank[1][:, m * 64:(m + 1) * 64], zr[0:64, 4, m * P:(m + 1) * P], ident[0:64, 0:64])
            last.then_inc(kt_ps, 1)

            pe.wait_ge(kt_ev, 3)
            pe.wait_ge(kt_ev_a, 3)
            pe.wait_ge(rlp_in, 128)
            for n in range(4):
                for k in range(4 * n, 4 * n + 4):
                    last = pe.transpose(bank[4 + n][:, (k % 4) * P:(k % 4 + 1) * P], rlp[k // 8][:, k % 8], ident)
                last.then_inc(xtp_ps, 1)
            for k in range(16):
                s, q = divmod(k, SP2)
                if k % 4 == 0:
                    pe.wait_ge((xtp_ev_v, xtp_ev_a)[k // 4 % 2], k // 8 + 1)
                h = bank[2 + s][:, 0:4 * PCN].rearrange("p (g n) -> p g n", g=4)
                for j in range(2):
                    last = pe.matmul(h, wc[:, s, j, q], xtp[:, k, :, j:j + PCN], start=(q == 0 and j == 0),
                                     stop=(q == SP2 - 1 and j == 1))
                if q == SP2 - 1:
                    last.then_inc(hp_ps, 1)
            pe.wait_ge(hp_ev, 1)
            hk = htp[:, 0, 0:4 * PCN].rearrange("p (a g n) -> p a g n", a=2, g=2)
            for g in range(2):
                last = pe.matmul(bank[0][:, 0:2 * PCN].rearrange("p (a n) -> p a n", a=2), w2pad[:, g], hk[:, :, g],
                                 start=g == 0, stop=g == 1)
            last.then_inc(w2p_ps, 1)
            pe.wait_ge(hp_ev, 2)
            for g in range(NKV):
                last = pe.matmul(bank[1][0:PCN, g * HD:(g + 1) * HD], htp[:, 1, g * PCN:(g + 1) * PCN], w2v,
                                 start=True, stop=True)
            last.then_inc(w2p_ps, 1)

            pe.wait_ge(w2p_ev, 3)
            for i in range(4):
                for m in range(8):
                    last = pe.matmul(bank[i][:, m * 2 * PC:(m + 1) * 2 * PC], qT[:, m, i * P:(i + 1) * P],
                                     kctp[:, m // 4].rearrange("p g n -> p (g n)"), start=True, stop=True)
                last.then_inc(cs_ps, 1)
            pe.wait_ge(vbd_in, 64)
            for i in range(4):
                pe.wait_ge(cs_sc, i + 1)
                if i >= 2:
                    pe.wait_ge(ct_ev, i - 1)
                for g in range(NKV):
                    last = pe.transpose(bank[4 + i % 2][:, g * P:(g + 1) * P], pc[i % 2][:, g * P:(g + 1) * P], ident)
                last.then_inc(ct_ps, 1)
                pe.wait_ge(ct_ev, i + 1)
                if i:
                    pe.wait_ge(co_ev, 2 * i)
                for g in range(NKV):
                    last = pe.matmul(bank[6 + g // 2][:, (g % 2) * 256:(g % 2 + 1) * 256], pcT[:, g * P:(g + 1) * P], vbd[:, g],
                                     start=True, stop=True)
                last.then_inc(co_ps, 1)

            pe.wait_ge(co_ev, 8)
            for gp in range(2):
                with pe.Fori(0, 2) as it:
                    g0 = it * 32 + gp * 64

                    def scores(u):
                        g2, i, br, c = UNITS[u]
                        if u % 16 == 0:
                            pe.wait_ge(qs_ready, it * 4 + (gp * 8 + 2 * c + 2))
                        if u >= 3:
                            pe.wait_ge(u_ex, g0 + (u - 2))
                        n = (i + 1) * P
                        pe.matmul(bank[u % 3][:, 0:n], qs[c][:, g2, i * P:(i + 1) * P], ktp[:, br, gp, 0:n],
                                  start=True, stop=True).then_inc(u_sc, 1)

                    scores(0)
                    scores(1)
                    for u in range(33):
                        if u + 2 < 32:
                            scores(u + 2)
                        if u < 32:
                            i = UNITS[u][1]
                            pe.wait_ge(u_ex, g0 + (u + 1))
                            if u >= 2:
                                pe.wait_ge(u_pt, g0 + (u - 1))
                            for k in range(i + 1):
                                last = pe.transpose(bank[3 + u % 2][:, k * P:(k + 1) * P], prob[:, u % 3, k * P:(k + 1) * P], ident)
                            last.then_inc(u_tp, 1)
                        if u >= 1:
                            v = u - 1
                            g2, i, br, c = UNITS[v]
                            pe.wait_ge(u_pt, g0 + (v + 1))
                            pe.wait_ge(u_fo, g0 + (v + 1))
                            col = (3 + 2 * br) * 256 + (gp * 2 + g2) * HD
                            for k in range(i + 1):
                                last = pe.matmul(bank[5 + v % 3][:, 0:HD], probT[:, v % 2, k * P:(k + 1) * P], kvr[:, k, col:col + HD],
                                                 start=k == 0, stop=k == i)
                            last.then_inc(u_pv, 1)
            for t in range(4):
                transpose_tile(pe, lambda t, k: att[:, t, k].rearrange("p g d -> p (g d)"), t, PAIRS, oT_ps, oT_ev, oz_ready)

            for w in range(2):
                pe.wait_ge(oT_ev[w], 4)
            pe.wait_ge(u_fo, 128 + 3)

            def step(b, c, scores=True, output=True):
                p, s2 = pb[1 - c], 1 - c
                groups = ([[(2056 + t * P, P, wk[:, s2, t, 256:512]) for t in range(4)],
                           [(2056 + WIN, TS, vn[0:TS, s2, 1]), (2576, NC, vcb[0:NC, s2])]]
                          + [[((4 * n + t) * P, P, kv[:, s2, 4 * n + t, 256:512]) for t in range(4)] for n in range(4)]
                          + [[(PAST, TS, vn[0:TS, s2, 0])]])

                def copied_out(n):
                    pe.wait_ge((e_pt_v, e_pt_a)[n % 2], (b - 1) * (4 - n % 2) + (n // 2 + 1))

                def turn_weights(n):
                    if n:
                        copied_out(n - 1)
                    pe.wait_ge(e_scl, b * 2 - (1 if n < 2 else 0))
                    for t, (col, rows, _) in enumerate(groups[n]):
                        last = pe.transpose(bank[7][0:rows, t * P:(t + 1) * P], p[:, col:col + rows], ident)
                    last.then_inc(e_pp, 1)

                def weigh(n):
                    copied_out(n)
                    if n == 0:
                        pe.wait_ge(c_stage, b)
                        pe.wait_ge(v_in[s2], (b - 1 - s2) * 24 + 48)
                        pe.wait_ge(vp_in[s2], (b - 1 - s2) * 128 + 256)
                        pe.wait_ge(e_oz, b * 4 - 3)
                    for t, (_, rows, v) in enumerate(groups[n]):
                        for g in range(2):
                            rhs = pt[0:rows, n % 4, t * P:(t + 1) * P].rearrange("p (q g m) -> p g q m", q=TS, g=2)[:, g]
                            last = pe.matmul(bank[5 + g][:, 0:64].rearrange("p (q m) -> p q m", q=TS), v[:, g * P:(g + 1) * P], rhs,
                                             start=n == 0 and t == 0, stop=n == 6)
                    if n == 6:
                        last.then_inc(e_pv, 1)

                def turn_keys(n):
                    if n == 0:
                        pe.wait_ge(win_in[c], (b - c) * 8 + 16)
                    if n == 1:
                        pe.wait_ge(kv_in[c], (b - c) * 128 + 256)
                    for g in range(2):
                        if n:
                            pe.wait_ge(e_te, b * 10 + (2 * n - 1 + g))
                        for t in range(4):
                            page = (n - 1) * 4 + t
                            if n == 0:
                                src = wk[:, c, t]
                            elif type(b) is int and b == 0:
                                src = early(page)
                            else:
                                src = kv[:, c, page]
                            last = pe.transpose(bank[3 + g][:, t * P:(t + 1) * P], src[:, g * P:(g + 1) * P], ident)
                    last.then_inc(e_tp, 1)

                if scores:
                    pe.wait_ge(q_stage, b + 1)
                    pe.wait_ge(e_cm, b + 1)
                    for g in range(2):
                        pe.matmul(bank[0][:, 0:NC], qb[:, c, g], kcT[:, bass.ds(b, 1), g].rearrange("p b n -> p (b n)"),
                                  start=g == 0, stop=g == 1)
                    for g in range(2):
                        last = pe.matmul(bank[0][:, 128:144].rearrange("p (s n) -> p s n", s=2), qb[:, c, g],
                                         kts[:, :, g, bass.ds(b * TS, TS)], start=g == 0, stop=g == 1)
                    last.then_inc(e_sc, 1)
                    turn_keys(0)
                for n in range(5):
                    if scores:
                        if n < 4:
                            turn_keys(n + 1)
                        pe.wait_ge(e_te, b * 10 + (2 * n + 2))
                        pe.wait_ge(e_ma, b * 5 + max(n, 1))
                        for g in range(2):
                            last = pe.matmul(s_bank[n][:, :], qb[:, c, g], ktb[n % 2][:, g], start=g == 0, stop=g == 1)
                        last.then_inc(e_s, 1)
                        if n == 1:
                            pe.wait_ge(e_cn, b + 1)
                            pe.matmul(bank[0][:, 256:256 + NC], quad, pcn, start=True, stop=True).then_inc(e_q4, 1)
                    if output:
                        for m in ((), (0, 1), (2, 3), (4, 5, 6, 7), ())[n]:
                            if m < 7:
                                turn_weights(m)
                            if m:
                                weigh(m - 1)

            sample_order(pe, step)

            pe.wait_ge(e_cm, NB + 1)
            pe.wait_ge(e_ma, 5 * NB + 1)
            pe.wait_ge(e_oz, 4 * NB + 1)
            pe.wait_ge(w_o_in, 256)
            for t in range(TT):
                r = ROWS[t]
                for nh in range(2):
                    n = 2 * t + nh
                    if n >= 8:
                        pe.wait_ge(o_free, 2 * TT + n - 7)
                    for m in range(8):
                        last = pe.matmul(bank[n % 8][0:r, :], oT[:, m, t * P:t * P + r], w_o[:, m, nh * 512:(nh + 1) * 512],
                                         start=m == 0, stop=m == 7)
                    last.then_inc(o2_ps, 1)



_INS = ["x_prompt", "x_sample", "state_conv", "cache_kv", "cache_win", "page_table", "conv_w_in", "conv_b_in", "conv_dw_w",
        "conv_dw_b", "conv_ln_g", "conv_ln_b", "conv_w_out", "nsa_w_in", "cmp_pe", "cmp_w1", "cmp_b1", "cmp_w2", "nsa_w_out",
        "ln_g", "ln_b"]
_OUTS = [(1, 512, 1024), (8, 8, 1024), (1, 1, 30, 2048), (1, 8, 30, 2048), (1, 1, 512, 4, 4, 64), (1, 8, 8, 4, 4, 64),
         (1, 1, 512, 2, 4, 64), (1, 8, 512, 2, 4, 64)]


def kernel(**inputs):
    import numpy as _np
    import concourse.bacc as _bacc
    from concourse import mybir as _mybir
    from concourse.bass_utils import run_bass_kernel_spmd as _run

    nc = _bacc.Bacc("TRN2", target_bir_lowering=False, num_devices=1)
    arrays, args = {}, []
    for name in _INS:
        a = _np.ascontiguousarray(inputs[name])
        arrays[f"in_{name}_dram"] = a
        args.append(nc.dram_tensor(f"in_{name}_dram", a.shape, _mybir.dt.from_np(a.dtype), kind="ExternalInput").ap())
    for i, shape in enumerate(_OUTS):
        args.append(nc.dram_tensor(f"out_{i}_dram", shape, _mybir.dt.float32, kind="ExternalOutput").ap())
    build_program(nc, *args)
    r = _run(nc, [arrays], core_ids=[0])
    return tuple(r.results[0][f"out_{i}_dram"] for i in range(len(_OUTS)))
```
